# Optimizing a Trainium2 kernel written in Bass

```python
import math
import jax
import jax.numpy as jnp
from jax import lax
import numpy as np

D_MODEL = 1024
BATCH = 1
SEQ = 512
DEPTH = 2
DEC_BATCH = 1
DEC_SEQ = 32
PAST_LEN = 512

CHUNK = 64
Q_BLOCK = 128
N_EVEN = (DEPTH + 1) // 2
N_ODD = DEPTH // 2
A_WIDTH = D_MODEL // 2
A_QK_DIM = 64
A_V_DIM = 2 * A_QK_DIM
A_HEADS = A_WIDTH // A_V_DIM
B_WIDTH = D_MODEL // 2
B_DK = 128
B_HEADS = B_WIDTH // B_DK
B_DV = B_WIDTH // B_HEADS
C_WIDTH = D_MODEL
C_DK = 128
C_DV = 128
C_HEADS = C_WIDTH // C_DK
CONV_W = 4
D_FF = 2816
EVEN_PROJ = 3 * A_WIDTH + 4 * B_WIDTH
ODD_PROJ = 4 * C_WIDTH + 2 * C_HEADS
NORM_EPS = 1e-6
DIFF_NORM_EPS = 1e-5

kernel_name = 'hybrid_streaming_encoder_step'

def rms_norm(x, gain, eps=NORM_EPS):
    x32 = x.astype(jnp.float32)
    y = x32 * lax.rsqrt(jnp.mean(x32 * x32, axis=-1, keepdims=True) + eps)
    return (y * gain.astype(jnp.float32)).astype(x.dtype)

def l2_normalize(x, eps=1e-6):
    x32 = x.astype(jnp.float32)
    return x32 * lax.rsqrt(jnp.sum(x32 * x32, axis=-1, keepdims=True) + eps)

def swiglu(h, w_in, w_out):
    gate, up = jnp.split(h @ w_in, 2, axis=-1)
    return (jax.nn.silu(gate) * up) @ w_out

def alibi_slopes():
    return 2.0 ** (-8.0 * jnp.arange(1, A_HEADS + 1, dtype=jnp.float32) / A_HEADS)

def to_chunks(x, size):
    b, t = x.shape[:2]
    x = x.reshape(b, t // size, size, *x.shape[2:])
    return jnp.moveaxis(jnp.moveaxis(x, 1, 0), 2, 3)

def from_chunks(x):
    x = jnp.moveaxis(jnp.moveaxis(x, 3, 2), 0, 1)
    b, nc, size = x.shape[:3]
    return x.reshape(b, nc * size, *x.shape[3:])

def diff_attention_block(q, k, v, q_pos, k_pos, lam, lam_init, gain):
    s = jnp.einsum('bqhmd,bkhmd->bhmqk', q, k).astype(jnp.float32) * (A_QK_DIM ** -0.5)
    dist = jnp.abs(q_pos[:, None] - k_pos[None, :]).astype(jnp.float32)
    visible = (k_pos[None, :] // CHUNK) <= (q_pos[:, None] // CHUNK)
    bias = jnp.where(visible, -alibi_slopes()[:, None, None] * dist, -jnp.inf)
    p = jax.nn.softmax(s + bias[None, :, None], axis=-1)
    p = p[:, :, 0] - lam * p[:, :, 1]
    o = jnp.einsum('bhqk,bkhe->bqhe', p.astype(v.dtype), v)
    return rms_norm(o, gain, DIFF_NORM_EPS) * (1.0 - lam_init)

def diff_attention_prompt(q, k, v, lam, lam_init, gain):
    b, t = q.shape[:2]
    nb = t // Q_BLOCK
    k_pos = jnp.arange(t, dtype=jnp.int32)
    q_blocks = jnp.moveaxis(q.reshape(b, nb, Q_BLOCK, A_HEADS, 2, A_QK_DIM), 1, 0)
    starts = jnp.arange(nb, dtype=jnp.int32) * Q_BLOCK

    def one_block(args):
        qb, st = args
        q_pos = st + jnp.arange(Q_BLOCK, dtype=jnp.int32)
        return diff_attention_block(qb, k, v, q_pos, k_pos, lam, lam_init, gain)

    o = lax.map(one_block, (q_blocks, starts))
    return jnp.moveaxis(o, 0, 1).reshape(b, t, A_HEADS, A_V_DIM)

def hgrn2_recurrence(q, k, v, log_f, s0):
    size = min(CHUNK, q.shape[1])
    incl = jnp.tril(jnp.ones((size, size), dtype=bool))

    def step(s, inp):
        qc, kc, vc, lfc = inp
        cb = jnp.cumsum(lfc, axis=2)
        rel = jnp.exp(jnp.where(incl[:, :, None], cb[:, :, :, None, :] - cb[:, :, None, :, :], -jnp.inf))
        scores = jnp.einsum('bhtd,bhsd,bhtsd->bhts', qc, kc, rel)
        o = scores @ vc + jnp.einsum('bhtd,bhde->bhte', qc * jnp.exp(cb), s)
        c_last = cb[:, :, -1:, :]
        s = jnp.exp(c_last[:, :, 0, :, None]) * s + jnp.einsum('bhsd,bhse->bhde', kc * jnp.exp(c_last - cb), vc)
        return s, o

    xs = tuple(to_chunks(a.astype(jnp.float32), size) for a in (q, k, v, log_f))
    s, o = lax.scan(step, s0.astype(jnp.float32), xs)
    return from_chunks(o), s

def gated_delta_recurrence(q, k, v, beta, g, s0):
    size = min(CHUNK, q.shape[1])
    strict = jnp.tril(jnp.ones((size, size), dtype=bool), -1)
    incl = jnp.tril(jnp.ones((size, size), dtype=bool))
    eye = jnp.eye(size, dtype=jnp.float32)

    def step(s, inp):
        qc, kc, vc, bc, gc = inp
        gam = jnp.cumsum(gc, axis=-1)
        diff = gam[..., :, None] - gam[..., None, :]
        d_strict = jnp.exp(jnp.where(strict, diff, -jnp.inf))
        d_incl = jnp.exp(jnp.where(incl, diff, -jnp.inf))
        kt = jnp.swapaxes(kc, -1, -2)
        m = eye + bc[..., :, None] * (kc @ kt) * d_strict
        w = lax.linalg.triangular_solve(m, kc * (bc * jnp.exp(gam))[..., None], left_side=True, lower=True, unit_diagonal=True)
        u = lax.linalg.triangular_solve(m, vc * bc[..., None], left_side=True, lower=True, unit_diagonal=True)
        v_new = u - w @ s
        o = (qc * jnp.exp(gam)[..., None]) @ s + ((qc @ kt) * d_incl) @ v_new
        g_last = gam[..., -1:]
        s = jnp.exp(g_last)[..., None] * s + jnp.swapaxes(kc * jnp.exp(g_last - gam)[..., None], -1, -2) @ v_new
        return s, o

    xs = tuple(to_chunks(a.astype(jnp.float32), size) for a in (q, k, v, beta, g))
    s, o = lax.scan(step, s0.astype(jnp.float32), xs)
    return from_chunks(o), s

def causal_conv(x, hist, w):
    t = x.shape[1]
    xp = jnp.concatenate([hist.astype(x.dtype), x], axis=1)
    y = sum(xp[:, j:j + t] * w[j] for j in range(CONV_W))
    return jax.nn.silu(y), xp[:, t:]

def even_mixer(h, layer, w_in, lam_vecs, diff_gain, lb, hgrn_gain, w_out, past_k, past_v, s0):
    b, t, _ = h.shape
    proj = h @ w_in
    sizes = [A_WIDTH, A_WIDTH, A_WIDTH, B_WIDTH, B_WIDTH, B_WIDTH]
    qa, ka, va, qb, fb, ib, gb = jnp.split(proj, list(np.cumsum(sizes)), axis=-1)
    qa = qa.reshape(b, t, A_HEADS, 2, A_QK_DIM)
    ka = ka.reshape(b, t, A_HEADS, 2, A_QK_DIM)
    va = va.reshape(b, t, A_HEADS, A_V_DIM)
    lam_init = 0.8 - 0.6 * math.exp(-0.3 * layer)
    lv = lam_vecs.astype(jnp.float32)
    lam = jnp.exp(jnp.sum(lv[0] * lv[1])) - jnp.exp(jnp.sum(lv[2] * lv[3])) + lam_init
    if past_k is None:
        oa = diff_attention_prompt(qa, ka, va, lam, lam_init, diff_gain)
    else:
        p_len = past_k.shape[1]
        k_all = jnp.concatenate([past_k.astype(ka.dtype), ka], axis=1)
        v_all = jnp.concatenate([past_v.astype(va.dtype), va], axis=1)
        q_pos = p_len + jnp.arange(t, dtype=jnp.int32)
        k_pos = jnp.arange(p_len + t, dtype=jnp.int32)
        oa = diff_attention_block(qa, k_all, v_all, q_pos, k_pos, lam, lam_init, diff_gain)
    f = lb + (1.0 - lb) * jax.nn.sigmoid(fb.astype(jnp.float32))
    heads = lambda a: a.reshape(b, t, B_HEADS, -1)
    ob, s_new = hgrn2_recurrence(heads(qb), heads(1.0 - f), heads(ib), heads(jnp.log(f)), s0)
    ob = rms_norm(ob, hgrn_gain) * jax.nn.silu(heads(gb).astype(jnp.float32))
    o = jnp.concatenate([oa.reshape(b, t, A_WIDTH).astype(h.dtype), ob.reshape(b, t, B_WIDTH).astype(h.dtype)], axis=-1)
    return o @ w_out, ka, va, s_new

def odd_mixer(h, w_in, conv_w, a_log, dt_bias, out_gain, w_out, conv_hist, s0):
    b, t, _ = h.shape
    proj = h @ w_in
    qkv, gate, a, bl = jnp.split(proj, [3 * C_WIDTH, 4 * C_WIDTH, 4 * C_WIDTH + C_HEADS], axis=-1)
    qkv, conv_new = causal_conv(qkv, conv_hist, conv_w)
    q, k, v = jnp.split(qkv, 3, axis=-1)
    q = l2_normalize(q.reshape(b, t, C_HEADS, C_DK)) * (C_DK ** -0.5)
    k = l2_normalize(k.reshape(b, t, C_HEADS, C_DK))
    v = v.reshape(b, t, C_HEADS, C_DV)
    beta = jax.nn.sigmoid(bl.astype(jnp.float32))
    g = -jnp.exp(a_log.astype(jnp.float32)) * jax.nn.softplus(a.astype(jnp.float32) + dt_bias.astype(jnp.float32))
    o, s_new = gated_delta_recurrence(q, k, v, beta, g, s0)
    o = rms_norm(o, out_gain) * jax.nn.silu(gate.reshape(b, t, C_HEADS, C_DV).astype(jnp.float32))
    return o.reshape(b, t, C_WIDTH).astype(h.dtype) @ w_out, s_new, conv_new

def setup_inputs(seed: int = 0) -> dict:
    key = jax.random.key(seed)
    ks = jax.random.split(key, 32)
    nrm = lambda k, shape, scale: scale * jax.random.normal(k, shape, jnp.float32)
    gain = lambda k, shape: 1.0 + 0.02 * jax.random.normal(k, shape, jnp.float32)
    dt = jnp.exp(jax.random.uniform(ks[24], (N_ODD, C_HEADS), jnp.float32, math.log(1e-3), math.log(1e-1)))
    return {
        'x_prompt': nrm(ks[0], (BATCH, SEQ, D_MODEL), 1.0),
        'x_sample': nrm(ks[1], (DEC_BATCH, DEC_SEQ, D_MODEL), 1.0),
        'cache_attn_k': nrm(ks[2], (N_EVEN, DEC_BATCH, PAST_LEN, A_HEADS, 2, A_QK_DIM), 1.0),
        'cache_attn_v': nrm(ks[3], (N_EVEN, DEC_BATCH, PAST_LEN, A_HEADS, A_V_DIM), 1.0),
        'state_hgrn': nrm(ks[4], (N_EVEN, DEC_BATCH, B_HEADS, B_DK, B_DV), 0.5),
        'state_delta': nrm(ks[5], (N_ODD, DEC_BATCH, C_HEADS, C_DK, C_DV), 0.1),
        'cache_conv': nrm(ks[6], (N_ODD, DEC_BATCH, CONV_W - 1, 3 * C_WIDTH), 1.0),
        'ffn1_norm': gain(ks[7], (DEPTH, D_MODEL)),
        'ffn1_w_in': nrm(ks[8], (DEPTH, D_MODEL, 2 * D_FF), D_MODEL ** -0.5),
        'ffn1_w_out': nrm(ks[9], (DEPTH, D_FF, D_MODEL), D_FF ** -0.5),
        'mix_norm': gain(ks[10], (DEPTH, D_MODEL)),
        'ffn2_norm': gain(ks[11], (DEPTH, D_MODEL)),
        'ffn2_w_in': nrm(ks[12], (DEPTH, D_MODEL, 2 * D_FF), D_MODEL ** -0.5),
        'ffn2_w_out': nrm(ks[13], (DEPTH, D_FF, D_MODEL), D_FF ** -0.5),
        'even_w_in': nrm(ks[14], (N_EVEN, D_MODEL, EVEN_PROJ), D_MODEL ** -0.5),
        'diff_lambda': nrm(ks[15], (N_EVEN, 4, A_QK_DIM), 0.1),
        'diff_norm': gain(ks[16], (N_EVEN, A_V_DIM)),
        'hgrn_lb_logits': nrm(ks[17], (N_EVEN + 1, B_WIDTH), 0.5),
        'hgrn_norm': gain(ks[18], (N_EVEN, B_DV)),
        'even_w_out': nrm(ks[19], (N_EVEN, A_WIDTH + B_WIDTH, D_MODEL), (A_WIDTH + B_WIDTH) ** -0.5),
        'odd_w_in': nrm(ks[20], (N_ODD, D_MODEL, ODD_PROJ), D_MODEL ** -0.5),
        'conv_w': nrm(ks[21], (N_ODD, CONV_W, 3 * C_WIDTH), CONV_W ** -0.5),
        'delta_A_log': jnp.log(jax.random.uniform(ks[22], (N_ODD, C_HEADS), jnp.float32, 1.0, 16.0)),
        'delta_dt_bias': dt + jnp.log(-jnp.expm1(-dt)),
        'delta_norm': gain(ks[23], (N_ODD, C_DV)),
        'odd_w_out': nrm(ks[25], (N_ODD, C_WIDTH, D_MODEL), C_WIDTH ** -0.5),
        'final_norm': gain(ks[26], (D_MODEL,)),
    }

def reference(x_prompt, x_sample, cache_attn_k, cache_attn_v, state_hgrn, state_delta, cache_conv,
              ffn1_norm, ffn1_w_in, ffn1_w_out, mix_norm, ffn2_norm, ffn2_w_in, ffn2_w_out,
              even_w_in, diff_lambda, diff_norm, hgrn_lb_logits, hgrn_norm, even_w_out,
              odd_w_in, conv_w, delta_A_log, delta_dt_bias, delta_norm, odd_w_out, final_norm):
    lower_bounds = jnp.cumsum(jax.nn.softmax(hgrn_lb_logits.astype(jnp.float32), axis=0), axis=0)

    def run(x, past_k, past_v, hgrn0, delta0, conv0):
        ks, vs, hs, ds, cs = [], [], [], [], []
        for layer in range(DEPTH):
            j = layer // 2
            x = x + 0.5 * swiglu(rms_norm(x, ffn1_norm[layer]), ffn1_w_in[layer], ffn1_w_out[layer])
            h = rms_norm(x, mix_norm[layer])
            if layer % 2 == 0:
                pk = None if past_k is None else past_k[j]
                pv = None if past_v is None else past_v[j]
                o, k, v, s = even_mixer(h, layer, even_w_in[j], diff_lambda[j], diff_norm[j], lower_bounds[j],
                                        hgrn_norm[j], even_w_out[j], pk, pv, hgrn0[j])
                ks.append(k)
                vs.append(v)
                hs.append(s.astype(x.dtype))
            else:
                o, s, c = odd_mixer(h, odd_w_in[j], conv_w[j], delta_A_log[j], delta_dt_bias[j], delta_norm[j],
                                    odd_w_out[j], conv0[j], delta0[j])
                ds.append(s.astype(x.dtype))
                cs.append(c)
            x = x + o
            x = x + 0.5 * swiglu(rms_norm(x, ffn2_norm[layer]), ffn2_w_in[layer], ffn2_w_out[layer])
        return (rms_norm(x, final_norm), jnp.stack(ks, axis=0), jnp.stack(vs, axis=0),
                jnp.stack(hs, axis=0), jnp.stack(ds, axis=0), jnp.stack(cs, axis=0))

    bp = x_prompt.shape[0]
    zeros_h = jnp.zeros((N_EVEN, bp, B_HEADS, B_DK, B_DV), jnp.float32)
    zeros_d = jnp.zeros((N_ODD, bp, C_HEADS, C_DK, C_DV), jnp.float32)
    zeros_c = jnp.zeros((N_ODD, bp, CONV_W - 1, 3 * C_WIDTH), x_prompt.dtype)
    y_prompt, k_p, v_p, h_p, d_p, c_p = run(x_prompt, None, None, zeros_h, zeros_d, zeros_c)
    y_sample, k_s, v_s, h_s, d_s, c_s = run(x_sample, cache_attn_k, cache_attn_v, state_hgrn, state_delta, cache_conv)
    return (y_prompt, y_sample, k_p, v_p, h_p, d_p, c_p, k_s, v_s, h_s, d_s, c_s)


_drawn_inputs = setup_inputs


def setup_inputs(seed=0):
    import zlib

    import numpy as np

    out = dict(_drawn_inputs(seed))
    spreads = {}
    factors = {'ffn1_norm': 2.738,
     'ffn2_norm': 5.383,
     'diff_norm': 3.552,
     'hgrn_norm': 5.364,
     'delta_norm': 40.926,
     'final_norm': 7.82}
    for name, (base, spread) in spreads.items():
        noise = np.random.default_rng([zlib.crc32(name.encode()), seed]).standard_normal(out[name].shape)
        drawn = base * np.exp(spread * noise) if base else spread * noise
        out[name] = jnp.asarray(drawn.astype(out[name].dtype))
    for name, factor in factors.items():
        out[name] = (out[name] * factor).astype(out[name].dtype)
    return out
```

```python
import math
from contextlib import ExitStack

import numpy as np

import concourse.bass as bass
from concourse import mybir

F32 = mybir.dt.float32
F32R = mybir.dt.float32r
I32 = mybir.dt.int32
ACT = mybir.ActivationFunctionType
ALU = mybir.AluOpType
AX_X = mybir.AxisListType.X
ds = bass.ds

P = 128
D = 1024
KT = D // P
SEQ = 512
DEC = 32
T = SEQ + DEC
TH = T // 2
PAST = 512
FF = 2816
FT = FF // P
UW = 256
FJ = FF // UW
PLAIN_PARTS = ((0, 8),)
OUT_PARTS = ((0, 8), (8, 16), (16, 22))
HEADS = 4
BLK = 128
NB = SEQ // BLK
LEVELS = 7
DEC_LEVELS = 5
CONV = 4
PADT = (CONV - 1) + SEQ + (CONV - 1) + DEC
NEG = -1.0e30
NORM_EPS = 1e-6
DIFF_EPS = 1e-5
LAM_INIT = 0.8 - 0.6 * math.exp(0.0)


class Sig:

    def __init__(self, ctx, nc, name, credit=0):
        self.sem = ctx.enter_context(nc.semaphore(name))
        self.credit = credit

    def at(self, count):
        value = count + self.credit
        return max(value, 0) if isinstance(value, int) else value

    def credit_by(self, eng):
        eng.sem_inc(self.sem, self.credit)


def level_masks():
    s = np.arange(P)[:, None]
    t = np.arange(P)[None, :]
    out = np.zeros((P, LEVELS, P), np.float32)
    for l in range(LEVELS):
        half = 1 << l
        out[:, l, :] = (s // (2 * half) == t // (2 * half)) & ((s // half) % 2 == 0) & ((t // half) % 2 == 1)
    return out


def constants():
    q = np.arange(P)[:, None]
    c = np.arange(-PAST, P)[None, :]
    alibi = -np.abs(q - c).astype(np.float32)
    alibi[(c >= 64) & (q < 64)] = NEG
    qs = np.arange(2 * DEC)[:, None] % DEC
    ks = np.arange(PAST + DEC)[None, :]
    alibi_dec = -np.abs(PAST + qs - ks).astype(np.float32)
    s = np.arange(P)[:, None]
    t = np.arange(P)[None, :]
    causal = np.where(t >= s, 0.0, NEG).astype(np.float32)
    slopes = np.tile(2.0 ** (-8.0 * np.arange(1, HEADS + 1, dtype=np.float32) / HEADS), (P, 1)).astype(np.float32)
    masks = level_masks()
    hmask = np.zeros((P, LEVELS, HEADS, 64), np.int32)
    for l in range(LEVELS):
        right = (np.arange(P) >> l) % 2 == 1
        hmask[:, l] = masks[:, l, right][:, None, :]
    return {
        "c_hmask": hmask.reshape(P, LEVELS * HEADS * 64),
        "c_ident": np.eye(P, dtype=np.float32),
        "c_levels": level_masks().reshape(P, LEVELS * P),
        "c_alibi": alibi.astype(np.float32),
        "c_alibi_dec": alibi_dec,
        "c_causal": causal,
        "c_tri": (t >= s).astype(np.float32),
        "c_slopes": slopes,
    }


class Overlay:

    def __init__(self, nc, start, end):
        self.nc, self.at, self.end = nc, start, end

    def buf(self, name, shape, dt=F32):
        size = 4 * int(np.prod(shape[1:]))
        where = self.at
        self.at += (size + 31) // 32 * 32
        assert self.at <= self.end, f"{name}: {self.at - self.end} bytes too many"
        return self.nc.alloc_sbuf_tensor_at(name, shape, dt, offset=where)



def program(nc, io, stop_after=None):
    with ExitStack() as ctx:
        build(nc, ctx, io)


def build(nc, ctx, io):
    def sb(name, shape, dt=F32):
        return ctx.enter_context(nc.sbuf_tensor(name, shape, dt))

    passed = {eng.engine: ctx.enter_context(nc.semaphore(f"passed_{name}"))
              for name, eng in (("act", nc.scalar), ("pool", nc.gpsimd), ("dve", nc.vector), ("pe", nc.tensor))}

    def set_apart(eng):
        eng.sem_inc(passed[eng.engine], 1)

    def sig(name, credit=0):
        return Sig(ctx, nc, name, credit)

    x = sb("x", [P, KT, T])
    raw = [sb(f"raw{s}", [P, KT, UW]) for s in range(2)]
    wh = [sb(f"wh{s}", [P, KT, UW], F32R) for s in range(2)]
    wl = [sb(f"wl{s}", [P, KT, UW], F32R) for s in range(2)]
    rstd = sb("rstd", [P, T])
    ssq = sb("ssq", [P, T])
    sq = [sb(f"sq{s}", [P, T]) for s in range(2)]
    ident = sb("ident", [P, P])
    ones = sb("ones", [P, P])
    COLS = 7 * KT + 7 * 24 + 8 + 3
    cols = sb("cols", [P, COLS])
    eps = sb("eps", [P, 2])
    adt = sb("adt", [P, 16])
    lamv = sb("lamv", [P, 8])
    ps = ctx.enter_context(nc.psum_tensor("ps", [P, 8, 512], F32))

    gain = lambda n, m: cols[:, m * 7 + n:m * 7 + n + 1]
    gain_at = lambda n, m: cols[:, ds(m * 7 + n, 1)]
    conv_col = lambda ch, r: cols[:, ds(7 * KT + ch * 7 + r, 1)]
    LB = 7 * KT + 7 * 24
    G3 = LB + 8

    def halves(slot):
        return ps[:, 2 * slot:2 * slot + 2, 0:TH]

    def two(ap):
        return ap.rearrange("p (a b) -> p a b", a=2)

    top = nc.sbuf_usable_end
    base = Overlay(nc, (nc.sbuf_base + 31) // 32 * 32, top)
    norm_at = Overlay(nc, base.at, top)
    xh = base.buf("xh", [P, KT, T], F32R)
    xl = base.buf("xl", [P, KT, T], F32R)
    norm_end = base.at
    arena = Overlay(nc, base.at, top)

    load = Overlay(nc, arena.at, top)
    xnat = load.buf("xnat", [P, NB, D])
    xnat_dec = load.buf("xnat_dec", [DEC, D])
    rows_gain = load.buf("rows_gain", [7, D])
    rows_conv = load.buf("rows_conv", [7, 3 * D])
    rows_lb = load.buf("rows_lb", [2, 512])
    rows_g3 = load.buf("rows_g3", [3, P])
    row_lam = load.buf("row_lam", [1, 272])
    lam_all = load.buf("lam_all", [P, 256])
    lam_prod = load.buf("lam_prod", [P, 2, 64])

    ffn = Overlay(nc, arena.at, top)
    hh = ffn.buf("hh", [P, FT, T], F32R)
    hl = ffn.buf("hl", [P, FT, T], F32R)
    gbuf = [ffn.buf(f"gbuf{s}", [P, T]) for s in range(2)]

    mixer = Overlay(nc, arena.at, top)
    mixh = mixer.buf("mixh", [P, KT, T], F32R)
    mixl = mixer.buf("mixl", [P, KT, T], F32R)

    av = Overlay(nc, mixer.at, top)
    att = av.buf("att", [P, 12, T])
    alibi = av.buf("alibi", [P, PAST + P])
    alibi_dec = av.buf("alibi_dec", [2 * DEC, PAST + DEC])
    slopes = av.buf("slopes", [P, HEADS])
    slope = av.buf("slope", [P, 1])
    qs = av.buf("qs", [P, T])
    ks = av.buf("ks", [P, T])
    vs = av.buf("vs", [P, T])
    qdec = av.buf("qdec", [P, 2 * DEC])
    pks = av.buf("pks", [P, NB, P])
    pvs = av.buf("pvs", [P, NB, P])
    pkt = av.buf("pkt", [P, PAST])
    kn = av.buf("kn", [P, NB, P])
    vn = av.buf("vn", [P, NB, P])
    kvd = av.buf("kvd", [DEC, 2, P])
    sc = [av.buf(f"sc{s}", [P, 2, 512]) for s in range(2)]
    scd = av.buf("scd", [2 * DEC, PAST + DEC])
    pt = [av.buf(f"pt{s}", [P, 512]) for s in range(2)]
    ptd = av.buf("ptd", [P, NB + 1, 2 * DEC])
    smax = [av.buf(f"smax{s}", [P, 8]) for s in range(2)]

    hv = Overlay(nc, mixer.at, top)
    hb = hv.buf("hb", [P, 16, T])
    kbuf = hv.buf("kbuf", [P, HEADS, T])
    hmask = hv.buf("hmask", [P, LEVELS * HEADS * 64], I32)
    hstate = [hv.buf(f"hstate{s}", [P, HEADS, P]) for s in range(2)]
    hlb = hv.buf("hlb", [P, 12])
    hw = Overlay(nc, norm_at.at, norm_end)
    hk = [hw.buf(f"hk{s}", [P, HEADS, BLK]) for s in range(2)]
    hq = [hw.buf(f"hq{s}", [P, HEADS, BLK]) for s in range(2)]
    hvb = [hw.buf(f"hvb{s}", [P, HEADS, BLK]) for s in range(2)]
    htot = [hw.buf(f"htot{s}", [P, 2 * HEADS * BLK]) for s in range(2)]
    hs = [hw.buf(f"hs{s}", [P, HEADS, BLK]) for s in range(2)]
    hkn = [hw.buf(f"hkn{s}", [P, HEADS, P]) for s in range(2)]
    hvn = [hw.buf(f"hvn{s}", [P, HEADS, P]) for s in range(2)]

    dv = Overlay(nc, mixer.at, top)
    db = dv.buf("db", [P, 24, T])
    dtail = dv.buf("dtail", [P, 24, 6])
    wab = dv.buf("wab", [P, KT, 16])
    wabh = dv.buf("wabh", [P, KT, 16], F32R)
    wabl = dv.buf("wabl", [P, KT, 16], F32R)
    gate_n = dv.buf("gate_n", [P, NB + 1, 16])
    lcol = dv.buf("lcol", [P, 8])
    gz = dv.buf("gz", [P, NB + 1, 8, 6])
    gcol = dv.buf("gcol", [P, NB + 1, 8])
    gamc = dv.buf("gamc", [P, NB + 1, 8])
    ngamc = dv.buf("ngamc", [P, NB + 1, 8])
    betac = dv.buf("betac", [P, NB + 1, 8])
    nexpa = dv.buf("nexpa", [P, 8])
    dv_in = Overlay(nc, dv.at, top)
    pre = [dv_in.buf(f"pre{s}", [P, PADT]) for s in range(2)]
    cacc = [dv_in.buf(f"cacc{s}", [P, PADT - 3]) for s in range(2)]
    dv_blk = Overlay(nc, dv.at, top)
    dstate = [dv_blk.buf(f"dstate{s}", [P, HEADS, P]) for s in range(2)]
    dlev = dv_blk.buf("dlev", [P, LEVELS, P])
    gate_at = Overlay(nc, arena.at, top)
    dgate = gate_at.buf("dgate", [P, KT, T])
    l2 = Overlay(nc, norm_at.at, norm_end)
    l2w = [l2.buf(f"l2w{s}", [P, HEADS, T]) for s in range(2)]
    dw_ = Overlay(nc, norm_at.at, norm_end)
    blockbuf = lambda name: dw_.buf(name, [P, HEADS, BLK])
    kst = blockbuf("kst")
    vst = blockbuf("vst")
    gst = blockbuf("gst")
    egam = blockbuf("egam")
    dW = blockbuf("dW")
    dBT = blockbuf("dBT")
    dBl = [blockbuf(f"dBl{s}") for s in range(2)]
    dQK = blockbuf("dQK")
    dX = blockbuf("dX")
    dU = blockbuf("dU")
    dZ = blockbuf("dZ")
    dkt = blockbuf("dkt")
    dqt = blockbuf("dqt")
    dvn = blockbuf("dvn")
    dkn = blockbuf("dkn")
    dr, dvv = dX, dZ
    causal = dw_.buf("causal", [P, P])
    tri = dw_.buf("tri", [P, P])
    kcoef = dw_.buf("kcoef", [P, HEADS])
    tail = Overlay(nc, norm_at.at, norm_end)
    tail_rows = tail.buf("tail_rows", [6, 3 * D])
    tri0 = dv_in.buf("tri0", [P, P])

    final = Overlay(nc, arena.at, top)
    yt = final.buf("yt", [P, KT, T])
    yout = [final.buf(f"yout{s}", [P, D]) for s in range(2)]

    raw_loaded = [sig(f"raw_loaded{s}") for s in range(2)]
    hi_done = sig("hi_done", 2)
    lo_done = sig("lo_done", 2)
    unit_done = sig("unit_done", 2)
    in_loaded = sig("in_loaded")
    vec_loaded = sig("vec_loaded")
    consts_set = sig("consts_set")
    xt_done = sig("xt_done")
    cols_psum = sig("cols_psum")
    cols_ready = sig("cols_ready")
    lam_psum = sig("lam_psum")
    lam_step = sig("lam_step")
    lam_exp = sig("lam_exp")
    x_ready = sig("x_ready")
    xh_ready = sig("xh_ready")
    xl_ready = sig("xl_ready")
    sq_ready = sig("sq_ready")
    ssq_done = sig("ssq_done")
    ssq_psum = sig("ssq_psum")
    rms_ready = sig("rms_ready")
    rstd_ready = sig("rstd_ready")
    gate_psum = sig("gate_psum")
    up_psum = sig("up_psum")
    gate_scaled = sig("gate_scaled", 2)
    gate_silu = sig("gate_silu")
    gate_rstd = sig("gate_rstd")
    h_made = sig("h_made", 2)
    hh_ready = sig("hh_ready")
    hl_ready = sig("hl_ready", 0)
    res_psum = sig("res_psum")
    proj_c0 = sig("proj_c0")
    proj_out = sig("proj_out", 4)
    gn_sq = sig("gn_sq")
    gn_psum = sig("gn_psum")
    gn_rms = sig("gn_rms")
    gn_step = sig("gn_step")
    gn_hi = sig("gn_hi")
    mix_ready = sig("mix_ready")
    at_tables = sig("at_tables")
    qdec_zero = sig("qdec_zero")
    pk_loaded = sig("pk_loaded")
    pv_loaded = sig("pv_loaded")
    staged = sig("staged")
    kv_t = sig("kv_t", 1)
    kn_ready = sig("kn_ready")
    vn_ready = sig("vn_ready")
    kv_stored = sig("kv_stored", 16)
    sc_psum = sig("sc_psum", 1)
    biased = sig("biased", 2)
    maxed = sig("maxed")
    nmax_ready = sig("nmax_ready")
    p_exp = sig("p_exp")
    comb = sig("comb")
    p_ready = sig("p_ready")
    pt_psum = sig("pt_psum", 2)
    pt_copied = sig("pt_copied", 2)
    o_psum = sig("o_psum", 2)
    o_copied = sig("o_copied", 2)
    hg_tables = sig("hg_tables")
    hg_gate = sig("hg_gate")
    hg_prep = sig("hg_prep")
    hg_staged = sig("hg_staged")
    hg_q = sig("hg_q", 1)
    hg_tot = sig("hg_tot")
    hg_k = sig("hg_k")
    hg_psum = sig("hg_psum")
    hg_s = sig("hg_s", 2)
    hg_t = sig("hg_t")
    hg_tn = sig("hg_tn")
    hg_o = sig("hg_o")
    hg_oc = sig("hg_oc", 1)
    hg_up = sig("hg_up", 1)
    hg_state = sig("hg_state", 1)
    hg_stored = sig("hg_stored")
    ab_loaded = sig("ab_loaded")
    ab_hi = sig("ab_hi")
    ab_lo = sig("ab_lo")
    ab_psum = sig("ab_psum")
    rs_psum = sig("rs_psum")
    gt = sig("gt")
    gta = sig("gta")
    gam_sum = sig("gam_sum")
    pre_ready = sig("pre_ready")
    tap0 = sig("tap0", 2)
    tap = sig("tap")
    conv_done = sig("conv_done", 2)
    gate_done = sig("gate_done")
    l2_sq = sig("l2_sq")
    l2_psum = sig("l2_psum")
    l2_rt = sig("l2_rt")
    l2_step = sig("l2_step")
    dl_tables = sig("dl_tables")
    dl_state_in = sig("dl_state_in")
    dl_staged = sig("dl_staged")
    dl_gam = sig("dl_gam")
    dl_kk = sig("dl_kk")
    dl_vk = sig("dl_vk", 1)
    dl_eg = sig("dl_eg")
    dl_w1 = sig("dl_w1")
    dl_w2 = sig("dl_w2")
    dl_w3 = sig("dl_w3")
    dl_bt = sig("dl_bt")
    dl_kq = sig("dl_kq", 1)
    dl_nat = sig("dl_nat", 1)
    dl_mask = sig("dl_mask")
    dl_z = sig("dl_z")
    dl_zc = sig("dl_zc")
    dl_xz = sig("dl_xz")
    dl_xu = sig("dl_xu", 1)
    dl_ks = sig("dl_ks")
    dl_r = sig("dl_r", 1)
    dl_vp = sig("dl_vp")
    dl_v = sig("dl_v", 1)
    dl_o = sig("dl_o", 1)
    dl_oc = sig("dl_oc", 1)
    dl_up = sig("dl_up")
    dl_s = sig("dl_s", 1)
    dl_stored = sig("dl_stored")
    tail_psum = sig("tail_psum")
    tail_copied = sig("tail_copied")
    tail_stored = sig("tail_stored")
    y_scaled = sig("y_scaled")
    y_psum = sig("y_psum")
    y_copied = sig("y_copied")
    y_stored = [sig(f"y_stored{s}") for s in range(2)]

    FFN_UNITS = 2 * FJ + 12
    U_FFN = [0, FFN_UNITS + 18, 2 * FFN_UNITS + 18, 3 * FFN_UNITS + 38]
    U_EVEN = FFN_UNITS
    U_ODD = 3 * FFN_UNITS + 18
    VECS = 17

    def split_hi(act, u, slot, kt=KT):
        act.wait_ge(raw_loaded[slot].sem, raw_loaded[slot].at(8 * (u - slot) + 16))
        set_apart(act)
        act.wait_ge(unit_done.sem, unit_done.at(u - 1))
        set_apart(act)
        nc.scalar.activation(wh[slot][:, 0:kt, :], raw[slot][:, 0:kt, :], ACT.Copy).then_inc(hi_done.sem, 1)

    def split_lo(dve, u, slot, kt=KT):
        dve.wait_ge(hi_done.sem, hi_done.at(u + 1))
        nc.vector.tensor_tensor(wl[slot][:, 0:kt, :], raw[slot][:, 0:kt, :], wh[slot][:, 0:kt, :].bitcast(F32),
                                ALU.subtract).then_inc(lo_done.sem, 1)

    def next_kt(parts, i):
        k0, k1 = parts[(i + 1) % len(parts)]
        return k1 - k0

    def mm3(pe_out, slot, k, c, rh, rl, rk, first, last):
        w_hi = wh[slot][:, k, c * P:(c + 1) * P]
        w_lo = wl[slot][:, k, c * P:(c + 1) * P]
        for a, (w, r) in enumerate(((w_hi, rh), (w_hi, rl), (w_lo, rh))):
            for b in range(2):
                ins = nc.tensor.matmul(ps[:, 2 * pe_out + b, 0:TH], w, r[:, rk, b * TH:(b + 1) * TH],
                                       start=first and a == 0, stop=last and a == 2)
        return ins

    def gain_of(n, m):
        return gain(n, m) if isinstance(m, int) else gain_at(n, m)

    def tile(buf, m):
        return buf[:, m, :] if isinstance(m, int) else buf[:, ds(m, 1), :].rearrange("p a t -> p (a t)")

    def feed_act(act, n, m, par, products=True):
        act.wait_ge(x_ready.sem, x_ready.at(8 * n + m + 1))
        set_apart(act)
        if products:
            nc.scalar.activation(tile(xh, m), tile(x, m), ACT.Copy, scale=gain_of(n, m)).then_inc(xh_ready.sem, 1)
        act.wait_ge(ssq_done.sem, ssq_done.at(8 * n + m - 1))
        set_apart(act)
        nc.scalar.activation(sq[par][:], tile(x, m), ACT.Square).then_inc(sq_ready.sem, 1)

    def feed_dve(dve, n, m):
        dve.wait_ge(xh_ready.sem, xh_ready.at(8 * n + m + 1))
        nc.vector.scalar_tensor_tensor(out=tile(xl, m), in0=tile(x, m), scalar=gain_of(n, m),
                                       in1=tile(xh, m).bitcast(F32), op0=ALU.mult,
                                       op1=ALU.subtract).then_inc(xl_ready.sem, 1)

    def feed_pool(pool, n):
        for m in range(KT):
            pool.wait_ge(sq_ready.sem, sq_ready.at(8 * n + m + 1))
            set_apart(pool)
            if m == 0:
                nc.gpsimd.tensor_copy(ssq[:], sq[0][:]).then_inc(ssq_done.sem, 1)
            else:
                pool.wait_ge(ssq_done.sem, ssq_done.at(8 * n + m))
                set_apart(pool)
                nc.gpsimd.tensor_tensor(ssq[:], ssq[:], sq[m % 2][:], ALU.add).then_inc(ssq_done.sem, 1)

    def stats_pe(pe, n):
        pe.wait_ge(ssq_done.sem, ssq_done.at(8 * (n + 1)))
        for b in range(2):
            ins = nc.tensor.matmul(ps[:, 6 + b, 0:TH], ones[:], ssq[:, b * TH:(b + 1) * TH], start=True, stop=True)
        ins.then_inc(ssq_psum.sem, 1)

    def stats_act(act, n):
        act.wait_ge(ssq_psum.sem, ssq_psum.at(n + 1))
        nc.scalar.activation(two(ssq[:]), halves(3), ACT.Sqrt, scale=1.0 / D, bias=eps[:, 0:1]).then_inc(rms_ready.sem, 1)

    def stats_dve(dve, n):
        dve.wait_ge(rms_ready.sem, rms_ready.at(n + 1))
        nc.vector.reciprocal(rstd[:], ssq[:]).then_inc(rstd_ready.sem, 1)

    def ffn_in_pe(pe, f, n):
        u0 = U_FFN[f]
        with pe.Fori(0, FJ) as j:
            for s in range(2):
                u = u0 + 2 * j + s
                pe.wait_ge(lo_done.sem, lo_done.at(u + 1))
                for c in range(2):
                    if s == 0:
                        pe.wait_ge(gate_scaled.sem, gate_scaled.at(2 * FJ * f + 2 * j + c - 1))
                    else:
                        if c == 1:
                            pe.wait_ge(rms_ready.sem, rms_ready.at(n + 1))
                        pe.wait_ge(h_made.sem, h_made.at(2 * FJ * f + 2 * j + c - 1))
                    for k in range(KT):
                        if s == 0 and c == 0:
                            pe.wait_ge(xl_ready.sem, xl_ready.at(8 * n + k + 1))
                        last = mm3(2 * s + c, s, k, c, xh, xl, k, k == 0, k == KT - 1)
                        if k == KT - 1 and c == 0:
                            last.then_inc((gate_psum if s == 0 else up_psum).sem, 1)
                last.then_inc(unit_done.sem, 1)

    def ffn_in_act(act, f, n):
        u0, g0 = U_FFN[f], 2 * FJ * f
        with act.Fori(0, FJ) as j:
            split_hi(act, u0 + 2 * j + 1, 1)
            for c in range(2):
                act.wait_ge(gate_scaled.sem, gate_scaled.at(g0 + 2 * j + c + 1))
                set_apart(act)
                nc.scalar.activation(gbuf[c][:], gbuf[c][:], ACT.Silu).then_inc(gate_silu.sem, 1)
            split_hi(act, u0 + 2 * j + 2, 0)
            for c in range(2):
                act.wait_ge(h_made.sem, h_made.at(g0 + 2 * j + c + 1))
                set_apart(act)
                nc.scalar.activation(tile(hh, 2 * j + c), sq[c][:], ACT.Copy).then_inc(hh_ready.sem, 1)

    def ffn_in_pool(pool, f, n):
        g0 = 2 * FJ * f
        pool.wait_ge(rstd_ready.sem, rstd_ready.at(n + 1))
        with pool.Fori(0, FJ) as j:
            for c in range(2):
                pool.wait_ge(gate_silu.sem, gate_silu.at(g0 + 2 * j + c + 1))
                set_apart(pool)
                nc.gpsimd.tensor_tensor(gbuf[c][:], gbuf[c][:], rstd[:], ALU.mult).then_inc(gate_rstd.sem, 1)

    def ffn_in_dve(dve, f, n):
        u0, g0 = U_FFN[f], 2 * FJ * f
        dve.wait_ge(rstd_ready.sem, rstd_ready.at(n + 1))
        with dve.Fori(0, FJ) as j:
            split_lo(dve, u0 + 2 * j + 1, 1)
            for c in range(2):
                if c == 0:
                    dve.wait_ge(gate_psum.sem, gate_psum.at(FJ * f + j + 1))
                else:
                    dve.wait_ge(unit_done.sem, unit_done.at(u0 + 2 * j + 1))
                nc.vector.tensor_tensor(two(gbuf[c][:]), halves(c), two(rstd[:]), ALU.mult).then_inc(gate_scaled.sem, 1)
            split_lo(dve, u0 + 2 * j + 2, 0)
            for c in range(2):
                dve.wait_ge(gate_rstd.sem, gate_rstd.at(g0 + 2 * j + c + 1))
                if c == 0:
                    dve.wait_ge(up_psum.sem, up_psum.at(FJ * f + j + 1))
                else:
                    dve.wait_ge(unit_done.sem, unit_done.at(u0 + 2 * j + 2))
                nc.vector.tensor_tensor(two(sq[c][:]), halves(2 + c), two(gbuf[c][:]), ALU.mult).then_inc(h_made.sem, 1)
            for c in range(2):
                dve.wait_ge(hh_ready.sem, hh_ready.at(g0 + 2 * j + c + 1))
                nc.vector.tensor_tensor(tile(hl, 2 * j + c), sq[c][:], tile(hh, 2 * j + c).bitcast(F32),
                                        ALU.subtract).then_inc(hl_ready.sem, 1)

    def out_pe(pe, u0, o, parts, rh, rl, n, src_ready):
        src_ready(pe)
        with pe.Fori(0, 2) as jj:
            for q in range(2):
                for i, (k0, k1) in enumerate(parts):
                    step = q * len(parts) + i
                    u = u0 + 2 * len(parts) * jj + step
                    slot = step % 2
                    pe.wait_ge(lo_done.sem, lo_done.at(u + 1))
                    for c in range(2):
                        if i == 0:
                            pe.wait_ge(x_ready.sem, x_ready.at(8 * n + 4 * jj + 2 * q + c - 3))
                        for k in range(k0, k1):
                            last = mm3(2 * q + c, slot, k - k0, c, rh, rl, k, k == 0, k == parts[-1][1] - 1)
                        if c == 0 and i == len(parts) - 1:
                            last.then_inc(res_psum.sem, 1)
                    last.then_inc(unit_done.sem, 1)

    def out_act(act, u0, parts, n, end):
        def pair(jj, q, end):
            for i in range(len(parts)):
                step = q * len(parts) + i
                if not (end and q == 1 and i == len(parts) - 1):
                    split_hi(act, u0 + 2 * len(parts) * jj + step + 1, (step + 1) % 2, next_kt(parts, i))
            for c in range(2):
                feed_act(act, n, 4 * jj + 2 * q + c, c, not end)
        if end:
            for jj in range(2):
                for q in range(2):
                    pair(jj, q, jj == 1)
        else:
            with act.Fori(0, 2) as jj:
                for q in range(2):
                    pair(jj, q, False)

    def out_dve(dve, u0, o, parts, n, scale, end):
        def pair(jj, q, end):
            for i in range(len(parts)):
                step = q * len(parts) + i
                if not (end and q == 1 and i == len(parts) - 1):
                    split_lo(dve, u0 + 2 * len(parts) * jj + step + 1, (step + 1) % 2, next_kt(parts, i))
            for c in range(2):
                m = 4 * jj + 2 * q + c
                if c == 0:
                    dve.wait_ge(res_psum.sem, res_psum.at(4 * o + 2 * jj + q + 1))
                else:
                    dve.wait_ge(unit_done.sem, unit_done.at(u0 + len(parts) * (2 * jj + q + 1)))
                nc.vector.scalar_tensor_tensor(out=two(tile(x, m)), in0=halves(2 * q + c), scalar=scale,
                                               in1=two(tile(x, m)), op0=ALU.mult, op1=ALU.add).then_inc(x_ready.sem, 1)
            if not end:
                for c in range(2):
                    feed_dve(dve, n, 4 * jj + 2 * q + c)
        if end:
            for jj in range(2):
                for q in range(2):
                    pair(jj, q, jj == 1)
        else:
            with dve.Fori(0, 2) as jj:
                for q in range(2):
                    pair(jj, q, False)

    def hidden_ready(f):
        return lambda pe: pe.wait_ge(hl_ready.sem, hl_ready.at(2 * FJ * (f + 1)))

    def stream(sp, u, slot, dst, src):
        sp.wait_ge(lo_done.sem, lo_done.at(u - 1))
        sp.dma_start(dst, src).then_inc(raw_loaded[slot].sem, 16)

    def stream_ffn(sp, f, w_in, w_out):
        u0 = U_FFN[f]
        wi = w_in.rearrange("(k p) n -> p k n", p=P)
        wo = w_out.rearrange("(k p) n -> p k n", p=P)
        with sp.Fori(0, FJ) as j:
            for s in range(2):
                stream(sp, u0 + 2 * j + s, s, raw[s][:], wi[:, :, ds(s * FF + UW * j, UW)])
        with sp.Fori(0, 2) as jj:
            for q in range(2):
                for i, (k0, k1) in enumerate(OUT_PARTS):
                    step = 3 * q + i
                    stream(sp, u0 + 2 * FJ + 6 * jj + step, step % 2, raw[step % 2][:, 0:k1 - k0, :],
                           wo[:, k0:k1, ds(UW * (2 * jj + q), UW)])

    def stream_plain(sp, u0, w, n_pairs, col=lambda j: 2 * UW * j):
        wi = w.rearrange("(k p) n -> p k n", p=P)
        with sp.Fori(0, n_pairs) as j:
            for s in range(2):
                stream(sp, u0 + 2 * j + s, s, raw[s][:], wi[:, :, ds(col(j) + s * UW, UW)])

    def proj_pe(pe, u0, i0, n, pairs):
        with pe.Fori(0, pairs) as j:
            for s in range(2):
                pe.wait_ge(lo_done.sem, lo_done.at(u0 + 2 * j + s + 1))
                for c in range(2):
                    pe.wait_ge(proj_out.sem, proj_out.at(i0 + 4 * j + 2 * s + c - 3))
                    if s == 1 and c == 0:
                        pe.wait_ge(rms_ready.sem, rms_ready.at(n + 1))
                    for k in range(KT):
                        if s == 0 and c == 0:
                            pe.wait_ge(xl_ready.sem, xl_ready.at(8 * n + k + 1))
                        last = mm3(2 * s + c, s, k, c, xh, xl, k, k == 0, k == KT - 1)
                    last.then_inc((proj_c0 if c == 0 else unit_done).sem, 1)

    def proj_act(act, u0, pairs):
        with act.Fori(0, pairs) as j:
            for s in range(2):
                split_hi(act, u0 + 2 * j + s + 1, 1 - s)

    def proj_dve(dve, u0, i0, n, pairs, dst):
        dve.wait_ge(rstd_ready.sem, rstd_ready.at(n + 1))
        with dve.Fori(0, pairs) as j:
            for s in range(2):
                split_lo(dve, u0 + 2 * j + s + 1, 1 - s)
                for c in range(2):
                    if c == 0:
                        dve.wait_ge(proj_c0.sem, proj_c0.at(i0 // 2 + 2 * j + s + 1))
                    else:
                        dve.wait_ge(unit_done.sem, unit_done.at(u0 + 2 * j + s + 1))
                    nc.vector.tensor_tensor(two(dst(4 * j + 2 * s + c)), halves(2 * s + c), two(rstd[:]),
                                            ALU.mult).then_inc(proj_out.sem, 1)

    def head_norm_act(act, g, src, work, src_ready, col, dst0, eps_i):
        src_ready(act)
        nc.scalar.activation(work, src, ACT.Square).then_inc(gn_sq.sem, 1)
        act.wait_ge(gn_psum.sem, gn_psum.at(g + 1))
        nc.scalar.activation(work.rearrange("p h (a b) -> p (h a) b", a=2), ps[:, :, 0:TH], ACT.Sqrt,
                             scale=1.0 / P, bias=eps[:, eps_i:eps_i + 1]).then_inc(gn_rms.sem, 1)
        act.wait_ge(gn_step.sem, gn_step.at(head_norm_steps(g)))
        nc.scalar.activation(mixh[:, dst0:dst0 + 4, :], work, ACT.Copy, scale=col).then_inc(gn_hi.sem, 1)

    def head_norm_steps(g):
        return 2 + 3 * g

    def head_norm_pe(pe, g, work, banks_free):
        pe.wait_ge(gn_sq.sem, gn_sq.at(g + 1))
        banks_free(pe)
        for h in range(HEADS):
            for b in range(2):
                ins = nc.tensor.matmul(ps[:, 2 * h + b, 0:TH], ones[:], work[:, h, b * TH:(b + 1) * TH],
                                       start=True, stop=True)
        ins.then_inc(gn_psum.sem, 1)

    def head_norm_dve(dve, g, src, work, col, dst0, gate=None):
        done = head_norm_steps(g)
        dve.wait_ge(gn_rms.sem, gn_rms.at(g + 1))
        first = done - (2 if gate is None else 3)
        nc.vector.reciprocal(work, work).then_inc(gn_step.sem, 1)
        dve.wait_ge(gn_step.sem, gn_step.at(first + 1))
        nc.vector.tensor_tensor(work, src, work, ALU.mult).then_inc(gn_step.sem, 1)
        if gate is not None:
            dve.wait_ge(gn_step.sem, gn_step.at(first + 2))
            nc.vector.tensor_tensor(work, work, gate, ALU.mult).then_inc(gn_step.sem, 1)
        dve.wait_ge(gn_hi.sem, gn_hi.at(g + 1))
        nc.vector.scalar_tensor_tensor(out=mixl[:, dst0:dst0 + 4, :], in0=work, scalar=col,
                                       in1=mixh[:, dst0:dst0 + 4, :].bitcast(F32), op0=ALU.mult,
                                       op1=ALU.subtract).then_inc(mix_ready.sem, 1)

    def width(b):
        return P * (b + 1)

    def att_pool(pool):
        ck = io["cache_attn_k"][0, 0].rearrange("(b p) h m d -> p b h (m d)", p=P)
        cv = io["cache_attn_v"][0, 0].rearrange("(b p) h d -> p b h d", p=P)
        nc.gpsimd.memset(qdec[:], 0.0).then_inc(qdec_zero.sem, 1)
        with pool.Fori(0, HEADS) as h:
            pool.wait_ge(kv_t.sem, kv_t.at(h))
            set_apart(pool)
            pool.dma_start(pks[:], ck[:, :, ds(h, 1), :].rearrange("p b a d -> p b (a d)")).then_inc(pk_loaded.sem, 16)
            pool.wait_ge(o_psum.sem, o_psum.at(5 * h))
            set_apart(pool)
            pool.dma_start(pvs[:], cv[:, :, ds(h, 1), :].rearrange("p b a d -> p b (a d)")).then_inc(pv_loaded.sem, 16)

    def att_act(act):
        act.dma_start(alibi[:], io["c_alibi"]).then_inc(at_tables.sem, 16)
        act.dma_start(alibi_dec[:], io["c_alibi_dec"]).then_inc(at_tables.sem, 16)
        act.dma_start(slopes[:], io["c_slopes"]).then_inc(at_tables.sem, 16)
        proj_act(act, U_EVEN, 3)
        act.wait_ge(proj_out.sem, proj_out.at(12))
        act.wait_ge(at_tables.sem, at_tables.at(48))
        act.wait_ge(qdec_zero.sem, qdec_zero.at(1))
        kp = io["k_prompt"][0, 0].rearrange("(b p) h m d -> p b h (m d)", p=P)
        vp = io["v_prompt"][0, 0].rearrange("(b p) h d -> p b h d", p=P)
        kd = io["k_sample"][0, 0].rearrange("t h m d -> t h (m d)")
        vd = io["v_sample"][0, 0]
        with act.Fori(0, HEADS) as h:
            act.wait_ge(biased.sem, biased.at(10 * h))
            set_apart(act)
            act.wait_ge(sc_psum.sem, sc_psum.at(5 * h))
            set_apart(act)
            nc.scalar.activation(qs[:], tile(att, h), ACT.Copy, scale=0.125)
            nc.scalar.activation(qdec[0:64, 0:DEC], att[0:64, ds(h, 1), SEQ:T].rearrange("p a t -> p (a t)"), ACT.Copy, scale=0.125)
            nc.scalar.activation(qdec[64:P, DEC:2 * DEC], att[64:P, ds(h, 1), SEQ:T].rearrange("p a t -> p (a t)"), ACT.Copy, scale=0.125)
            nc.scalar.activation(ks[:], tile(att, h + 4), ACT.Copy)
            nc.scalar.activation(slope[:], slopes[:, ds(h, 1)], ACT.Copy)
            nc.scalar.activation(vs[:], tile(att, h + 8), ACT.Copy).then_inc(staged.sem, 1)
            act.wait_ge(kv_t.sem, kv_t.at(h + 1))
            set_apart(act)
            act.wait_ge(kv_stored.sem, kv_stored.at(64 * h))
            set_apart(act)
            nc.scalar.activation(kn[:].rearrange("p b d -> p (b d)"), ps[:, 4, :], ACT.Copy)
            nc.scalar.activation(kvd[:].rearrange("p b d -> p (b d)"), ps[0:DEC, 7, 0:2 * P], ACT.Copy).then_inc(kn_ready.sem, 1)
            act.wait_ge(kn_ready.sem, kn_ready.at(h + 1))
            set_apart(act)
            act.wait_ge(vn_ready.sem, vn_ready.at(h + 1))
            set_apart(act)
            for src, dst in ((kn[:], kp), (vn[:], vp)):
                act.dma_start(dst[:, :, ds(h, 1), :].rearrange("p b a d -> p b (a d)"), src).then_inc(kv_stored.sem, 16)
            for i, dst in enumerate((kd, vd)):
                act.dma_start(dst[:, ds(h, 1), :].rearrange("t a d -> t (a d)"), kvd[:, i, :]).then_inc(kv_stored.sem, 16)

            def exps(b):
                act.wait_ge(nmax_ready.sem, nmax_ready.at(5 * h + b + 1))
                set_apart(act)
                if b == NB:
                    nc.scalar.activation(scd[:], scd[:], ACT.Exp, bias=smax[0][0:2 * DEC, 2:3],
                                         accum_out=smax[0][0:2 * DEC, 4:5]).then_inc(p_exp.sem, 1)
                    return
                for m in range(2):
                    ins = nc.scalar.activation(sc[b % 2][:, m, 0:width(b)], sc[b % 2][:, m, 0:width(b)], ACT.Exp,
                                               bias=smax[b % 2][:, 2 + m:3 + m], accum_out=smax[b % 2][:, 4 + m:5 + m])
                ins.then_inc(p_exp.sem, 1)

            def copy_pt(b):
                act.wait_ge(pt_psum.sem, pt_psum.at(5 * h + b + 1))
                set_apart(act)
                act.wait_ge(o_psum.sem, o_psum.at(5 * h + b - 1))
                set_apart(act)
                if b == NB:
                    nc.scalar.activation(ptd[:].rearrange("p b q -> p (b q)")[:, 0:NB * 2 * DEC], ps[:, 4, 0:NB * 2 * DEC], ACT.Copy)
                    nc.scalar.activation(ptd[0:DEC, NB, :], ps[0:DEC, 4, NB * 2 * DEC:(NB + 1) * 2 * DEC], ACT.Copy).then_inc(pt_copied.sem, 1)
                    return
                nc.scalar.activation(pt[b % 2][:, 0:width(b)], ps[:, 4 + b % 2, 0:width(b)], ACT.Copy).then_inc(pt_copied.sem, 1)

            exps(0)
            exps(1)
            copy_pt(0)
            exps(2)
            copy_pt(1)
            exps(3)
            copy_pt(2)
            exps(4)
            copy_pt(3)
            copy_pt(4)
            act.wait_ge(o_psum.sem, o_psum.at(5 * h + 4))
            set_apart(act)
            nc.scalar.activation(att[:, ds(h, 1), 0:SEQ].rearrange("p a t -> p (a t)"), ps[:, 6, :], ACT.Copy)
            act.wait_ge(o_psum.sem, o_psum.at(5 * h + 5))
            set_apart(act)
            nc.scalar.activation(att[:, ds(h, 1), SEQ:T].rearrange("p a t -> p (a t)"), ps[:, 7, 0:DEC], ACT.Copy).then_inc(o_copied.sem, 1)
        head_norm_act(act, 0, att[:, 0:4, :], att[:, 8:12, :], lambda e: e.wait_ge(o_copied.sem, o_copied.at(HEADS)), lamv[:, 6:7], 0, 1)

    def att_dve(dve):
        proj_dve(dve, U_EVEN, 0, 1, 3, lambda i: tile(att, i))
        dve.wait_ge(at_tables.sem, at_tables.at(48))
        with dve.Fori(0, HEADS) as h:
            dve.wait_ge(kv_t.sem, kv_t.at(h + 1))
            dve.wait_ge(kv_stored.sem, kv_stored.at(64 * h))
            nc.vector.tensor_copy(vn[:].rearrange("p b d -> p (b d)"), ps[:, 5, :])
            nc.vector.tensor_copy(pkt[:], ps[:, 6, :]).then_inc(vn_ready.sem, 1)

            def softmax_in(b):
                dve.wait_ge(sc_psum.sem, sc_psum.at(5 * h + b + 1))
                dve.wait_ge(pt_psum.sem, pt_psum.at(5 * h + b - 1))
                p = b % 2
                if b == NB:
                    for i, (lo, hi) in enumerate(((0, PAST), (PAST, PAST + DEC))):
                        nc.vector.scalar_tensor_tensor(out=scd[:, lo:hi], in0=alibi_dec[:, lo:hi], scalar=slope[0:2 * DEC, :],
                                                       in1=ps[0:2 * DEC, i, 0:hi - lo], op0=ALU.mult, op1=ALU.add).then_inc(biased.sem, 1)
                    dve.wait_ge(biased.sem, biased.at(10 * h + 10))
                    nc.vector.reduce_max(smax[0][0:2 * DEC, 0:1], scd[:], AX_X).then_inc(maxed.sem, 1)
                    dve.wait_ge(maxed.sem, maxed.at(5 * h + b + 1))
                    nc.vector.tensor_scalar(smax[0][0:2 * DEC, 2:3], smax[0][0:2 * DEC, 0:1], -1.0, None, ALU.mult).then_inc(nmax_ready.sem, 1)
                    return
                w = width(b)
                for m in range(2):
                    nc.vector.scalar_tensor_tensor(out=sc[p][:, m, 0:w], in0=alibi[:, PAST - P * b:PAST + P], scalar=slope[:],
                                                   in1=ps[:, 2 * p + m, 0:w], op0=ALU.mult, op1=ALU.add).then_inc(biased.sem, 1)
                dve.wait_ge(biased.sem, biased.at(10 * h + 2 * b + 2))
                nc.vector.reduce_max(smax[p][:, 0:2], sc[p][:, :, 0:w], AX_X).then_inc(maxed.sem, 1)
                dve.wait_ge(maxed.sem, maxed.at(5 * h + b + 1))
                nc.vector.tensor_scalar(smax[p][:, 2:4], smax[p][:, 0:2], -1.0, None, ALU.mult).then_inc(nmax_ready.sem, 1)

            def combine(b):
                dve.wait_ge(p_exp.sem, p_exp.at(5 * h + b + 1))
                p, w, c0 = b % 2, width(b), 14 * h + 3 * b
                if b == NB:
                    nc.vector.reciprocal(smax[0][0:2 * DEC, 6:7], smax[0][0:2 * DEC, 4:5]).then_inc(comb.sem, 1)
                    dve.wait_ge(comb.sem, comb.at(c0 + 1))
                    nc.vector.tensor_tensor(smax[0][0:2 * DEC, 7:8], smax[0][0:2 * DEC, 6:7], lamv[0:2 * DEC, 5:6], ALU.mult).then_inc(comb.sem, 1)
                    dve.wait_ge(comb.sem, comb.at(c0 + 2))
                    nc.vector.tensor_scalar(scd[:], scd[:], smax[0][0:2 * DEC, 7:8], None, ALU.mult).then_inc(p_ready.sem, 1)
                    return
                nc.vector.reciprocal(smax[p][:, 6:8], smax[p][:, 4:6]).then_inc(comb.sem, 1)
                dve.wait_ge(comb.sem, comb.at(c0 + 1))
                nc.vector.tensor_scalar(smax[p][:, 7:8], smax[p][:, 7:8], lamv[:, 4:5], None, ALU.mult).then_inc(comb.sem, 1)
                dve.wait_ge(comb.sem, comb.at(c0 + 2))
                nc.vector.tensor_scalar(sc[p][:, 1, 0:w], sc[p][:, 1, 0:w], smax[p][:, 7:8], None, ALU.mult).then_inc(comb.sem, 1)
                dve.wait_ge(comb.sem, comb.at(c0 + 3))
                nc.vector.scalar_tensor_tensor(out=sc[p][:, 0, 0:w], in0=sc[p][:, 0, 0:w], scalar=smax[p][:, 6:7],
                                               in1=sc[p][:, 1, 0:w], op0=ALU.mult, op1=ALU.add).then_inc(p_ready.sem, 1)

            softmax_in(0)
            softmax_in(1)
            for b in range(NB + 1):
                combine(b)
                if b + 2 <= NB:
                    softmax_in(b + 2)
        head_norm_dve(dve, 0, att[:, 0:4, :], att[:, 8:12, :], lamv[:, 6:7], 0)

    def att_pe(pe):
        proj_pe(pe, U_EVEN, 0, 1, 3)
        pe.wait_ge(proj_out.sem, proj_out.at(12))
        with pe.Fori(0, HEADS) as h:
            pe.wait_ge(staged.sem, staged.at(h + 1))
            pe.wait_ge(pk_loaded.sem, pk_loaded.at(16 * h + 16))
            pe.wait_ge(pt_copied.sem, pt_copied.at(5 * h))
            pe.wait_ge(o_copied.sem, o_copied.at(h))
            for b in range(NB):
                nc.tensor.transpose(ps[:, 4, b * P:(b + 1) * P], ks[:, b * P:(b + 1) * P], ident[:])
            for b in range(NB):
                nc.tensor.transpose(ps[:, 5, b * P:(b + 1) * P], vs[:, b * P:(b + 1) * P], ident[:])
            for b in range(NB):
                nc.tensor.transpose(ps[:, 6, b * P:(b + 1) * P], pks[:, b, :], ident[:])
            nc.tensor.transpose(ps[0:DEC, 7, 0:P], ks[:, SEQ:T], ident[:])
            nc.tensor.transpose(ps[0:DEC, 7, P:2 * P], vs[:, SEQ:T], ident[:]).then_inc(kv_t.sem, 1)

            def scores(b):
                pe.wait_ge(biased.sem, biased.at(10 * h + max(0, 2 * b - 2)))
                if b == NB:
                    pe.wait_ge(vn_ready.sem, vn_ready.at(h + 1))
                    nc.tensor.matmul(ps[0:2 * DEC, 0, :], qdec[:], pkt[:], start=True, stop=True)
                    nc.tensor.matmul(ps[0:2 * DEC, 1, 0:DEC], qdec[:], ks[:, SEQ:T], start=True, stop=True).then_inc(sc_psum.sem, 1)
                    return
                for m in range(2):
                    ins = nc.tensor.matmul(ps[:, 2 * (b % 2) + m, 0:width(b)], qs[64 * m:64 * m + 64, b * P:(b + 1) * P],
                                           ks[64 * m:64 * m + 64, 0:width(b)], start=True, stop=True)
                ins.then_inc(sc_psum.sem, 1)

            def transpose_p(b):
                pe.wait_ge(p_ready.sem, p_ready.at(5 * h + b + 1))
                pe.wait_ge(pt_copied.sem, pt_copied.at(5 * h + b - 1))
                if b == NB:
                    set_apart(pe)
                if b == 0:
                    pe.wait_ge(kn_ready.sem, kn_ready.at(h + 1))
                if b == 1:
                    pe.wait_ge(vn_ready.sem, vn_ready.at(h + 1))
                if b == NB:
                    for kb in range(NB):
                        nc.tensor.transpose(ps[:, 4, kb * 2 * DEC:(kb + 1) * 2 * DEC], scd[:, kb * P:(kb + 1) * P], ident[0:64, 0:64])
                    nc.tensor.transpose(ps[0:DEC, 4, NB * 2 * DEC:(NB + 1) * 2 * DEC], scd[:, PAST:PAST + DEC],
                                        ident[0:64, 0:64]).then_inc(pt_psum.sem, 1)
                    return
                for kb in range(b + 1):
                    ins = nc.tensor.transpose(ps[:, 4 + b % 2, kb * P:(kb + 1) * P], sc[b % 2][:, 0, kb * P:(kb + 1) * P], ident[:])
                ins.then_inc(pt_psum.sem, 1)

            def values(b):
                pe.wait_ge(pt_copied.sem, pt_copied.at(5 * h + b + 1))
                if b == 0:
                    pe.wait_ge(vn_ready.sem, vn_ready.at(h + 1))
                if b == NB:
                    pe.wait_ge(pv_loaded.sem, pv_loaded.at(16 * h + 16))
                    pe.wait_ge(kn_ready.sem, kn_ready.at(h + 1))
                    for kb in range(NB):
                        for m in range(2):
                            nc.tensor.matmul(ps[:, 7, 0:DEC], pvs[:, kb, :], ptd[:, kb, m * DEC:(m + 1) * DEC],
                                             start=kb == 0 and m == 0, stop=False)
                    for m in range(2):
                        ins = nc.tensor.matmul(ps[:, 7, 0:DEC], kvd[:, 1, :], ptd[0:DEC, NB, m * DEC:(m + 1) * DEC],
                                               start=False, stop=m == 1)
                    ins.then_inc(o_psum.sem, 1)
                    return
                for kb in range(b + 1):
                    ins = nc.tensor.matmul(ps[:, 6, b * P:(b + 1) * P], vn[:, kb, :], pt[b % 2][:, kb * P:(kb + 1) * P],
                                           start=kb == 0, stop=kb == b)
                ins.then_inc(o_psum.sem, 1)

            scores(0)
            scores(1)
            transpose_p(0)
            scores(2)
            values(0)
            transpose_p(1)
            scores(3)
            values(1)
            transpose_p(2)
            scores(4)
            values(2)
            transpose_p(3)
            values(3)
            transpose_p(4)
            values(4)
        head_norm_pe(pe, 0, att[:, 8:12, :], lambda e: e.wait_ge(o_copied.sem, o_copied.at(HEADS)))

    H_EV = 2 * (LEVELS + 1)

    def spans(buf, n, half):
        v = buf[:] if n == BLK else buf[:, :, 0:n]
        return v.rearrange("p h (x two f) -> p h x two f", two=2, f=half)

    def tot_off(l):
        return HEADS * BLK * 2 - (HEADS * BLK * 2 >> l)

    def level_total(a, n, l):
        return htot[a][:, tot_off(l):tot_off(l) + HEADS * n // (1 << l)]

    class HBlock:

        def __init__(self, i):
            self.dec = i is None
            self.blocks = (0,) if self.dec else (0, 1)
            self.n = DEC if self.dec else BLK
            self.levels = DEC_LEVELS if self.dec else LEVELS
            self.ev0 = 2 * H_EV if self.dec else H_EV * i
            self.lv0 = 4 * LEVELS if self.dec else 2 * LEVELS * i
            self.blk0 = NB if self.dec else 2 * i
            self.state = hstate[1] if self.dec else hstate[0]

        def ev(self, lev, a):
            return self.ev0 + len(self.blocks) * lev + a + 1

        def lv(self, l, a):
            return self.lv0 + len(self.blocks) * l + a + 1

        def tokens(self, buf, c0, a):
            if self.dec:
                return buf[:, c0:c0 + HEADS, SEQ:T]
            return buf[:, c0:c0 + HEADS, ds((self.blk0 + a) * BLK, BLK)]

    def hgrn_stage_act(act, hg):
        for a in hg.blocks:
            act.wait_ge(hg_q.sem, hg_q.at(hg.ev(-1, a) if hg.dec else hg.ev0))
            set_apart(act)
            act.wait_ge(hg_up.sem, hg_up.at(hg.blk0))
            set_apart(act)
            nc.scalar.activation(hk[a][:, :, 0:hg.n], hg.tokens(kbuf, 0, a), ACT.Copy)
            nc.scalar.activation(level_total(a, hg.n, 0).rearrange("p (h t) -> p h t", h=HEADS), hg.tokens(hb, 4, a), ACT.Copy)
            nc.scalar.activation(hvb[a][:, :, 0:hg.n], hg.tokens(hb, 8, a), ACT.Copy).then_inc(hg_staged.sem, 1)

    def hgrn_block_act(act, hg):
        hgrn_stage_act(act, hg)
        n = hg.n
        for a in hg.blocks:
            act.wait_ge(hg_t.sem, hg_t.at(hg.blk0 + a + 1))
            set_apart(act)
            nc.scalar.activation(hkn[a][0:n], ps[0:n, 4 + a, :].rearrange("p (h d) -> p h d", h=HEADS), ACT.Copy)
            nc.scalar.activation(hvn[a][0:n], ps[0:n, 6 + a, :].rearrange("p (h d) -> p h d", h=HEADS), ACT.Copy).then_inc(hg_tn.sem, 1)
        for a in hg.blocks:
            act.wait_ge(hg_o.sem, hg_o.at(hg.blk0 + a + 1))
            set_apart(act)
            nc.scalar.activation(hg.tokens(hb, 0, a), ps[:, 4 + a, 0:HEADS * n].rearrange("p (h t) -> p h t", h=HEADS),
                                 ACT.Copy).then_inc(hg_oc.sem, 1)

    def hgrn_block_pool(pool, hg):
        for l in range(hg.levels):
            half = 1 << l
            for a in hg.blocks:
                if l == 0:
                    pool.wait_ge(hg_staged.sem, hg_staged.at(hg.blk0 + a + 1))
                    set_apart(pool)
                else:
                    pool.wait_ge(hg_k.sem, hg_k.at(hg.lv(l - 1, a)))
                    set_apart(pool)
                nblk = HEADS * hg.n // (2 * half)
                t = level_total(a, hg.n, l).rearrange("p (x two) -> p x two", two=2)
                nc.gpsimd.tensor_tensor(level_total(a, hg.n, l + 1), t[:, :, 0], t[:, :, 1], ALU.mult).then_inc(hg_tot.sem, 1)
                pool.wait_ge(hg_psum.sem, hg_psum.at(hg.ev(l + 1, a)))
                set_apart(pool)
                left = spans(hk[a], hg.n, half)[:, :, :, 0, :]
                right_tot = t.rearrange("p (h x) two -> p h x two", h=HEADS)[:, :, :, 1:2].broadcast_to([P, HEADS, nblk // HEADS, half])
                nc.gpsimd.tensor_tensor(left, left, right_tot, ALU.mult).then_inc(hg_k.sem, 1)

    def hgrn_block_dve(dve, hg):
        n = hg.n
        for a in hg.blocks:
            dve.wait_ge(hg_staged.sem, hg_staged.at(hg.blk0 + a + 1))
            nc.vector.tensor_tensor(hq[a][:, :, 0:n], hg.tokens(hb, 0, a), hg.tokens(hb, 4, a), ALU.mult).then_inc(hg_q.sem, 1)
        for a in hg.blocks:
            dve.wait_ge(hg_psum.sem, hg_psum.at(hg.ev(0, a)))
            nc.vector.tensor_tensor(hs[a][0:n, :, 0:n], ps[0:n, 2 * a, 0:HEADS * n].rearrange("p (h t) -> p h t", h=HEADS),
                                    ident[0:n, 0:n].unsqueeze(1).broadcast_to([n, HEADS, n]), ALU.mult).then_inc(hg_s.sem, 1)
        for l in range(hg.levels):
            half = 1 << l
            for a in hg.blocks:
                dve.wait_ge(hg_psum.sem, hg_psum.at(hg.ev(l + 1, a)))
                if l:
                    dve.wait_ge(hg_tot.sem, hg_tot.at(hg.lv(l - 1, a)))
                dve.wait_ge(hg_q.sem, hg_q.at(hg.ev(l, a)))
                t = level_total(a, n, l).rearrange("p (h x two) -> p h x two", h=HEADS, two=2)
                nblk = n // (2 * half)
                right = spans(hq[a], n, half)[:, :, :, 1, :]
                nc.vector.tensor_tensor(right, right, t[:, :, :, 0:1].broadcast_to([P, HEADS, nblk, half]),
                                        ALU.mult).then_inc(hg_q.sem, 1)
                dve.wait_ge(hg_s.sem, hg_s.at(hg.ev(l, a)))
                set_apart(dve)
                mask = hmask[0:n, l * HEADS * 64:(l + 1) * HEADS * 64].rearrange("p (h t) -> p h t", h=HEADS)[:, :, 0:n // 2]
                src = ps[0:n, 2 * a + (l + 1) % 2, 0:HEADS * n // 2].rearrange("p (h t) -> p h t", h=HEADS)
                if n == BLK:
                    out = spans_p(hs[a], n, half)[:, :, 1, :]
                    nc.vector.copy_predicated(out, mask.rearrange("p h (x f) -> p (h x) f", f=half),
                                              src.rearrange("p h (x f) -> p (h x) f", f=half)).then_inc(hg_s.sem, 1)
                else:
                    for h in range(HEADS):
                        out = hs[a][0:n, h, 0:n].rearrange("p (x two f) -> p x two f", two=2, f=half)[:, :, 1, :]
                        ins = nc.vector.copy_predicated(out, mask[:, h, :].rearrange("p (x f) -> p x f", f=half),
                                                        src[:, h, :].rearrange("p (x f) -> p x f", f=half))
                    ins.then_inc(hg_s.sem, 1)
        for a in hg.blocks:
            tot = level_total(a, n, hg.levels)
            if hg.dec:
                st0 = 8
            else:
                st0 = 2 * hg.blk0
            dve.wait_ge(hg_o.sem, hg_o.at(hg.blk0 + a + 1))
            dve.wait_ge(hg_tot.sem, hg_tot.at(hg.lv(hg.levels - 1, a)))
            nc.vector.tensor_tensor(hg.state[:], hg.state[:], tot.unsqueeze(2).broadcast_to([P, HEADS, P]), ALU.mult).then_inc(hg_state.sem, 1)
            dve.wait_ge(hg_state.sem, hg_state.at(st0 + 2 * a + 1))
            dve.wait_ge(hg_up.sem, hg_up.at(hg.blk0 + a + 1))
            nc.vector.tensor_tensor(hg.state[:], hg.state[:], ps[:, 6 + a, :].rearrange("p (h e) -> p h e", h=HEADS),
                                    ALU.add).then_inc(hg_state.sem, 1)

    def spans_p(buf, n, half):
        return buf[0:n].rearrange("p h (x two f) -> p (h x) two f", two=2, f=half)

    def hgrn_block_pe(pe, hg):
        n = hg.n
        for a in hg.blocks:
            pe.wait_ge(hg_staged.sem, hg_staged.at(hg.blk0 + a + 1))
            pe.wait_ge(hg_s.sem, hg_s.at(hg.ev0))
            for h in range(HEADS):
                ins = nc.tensor.matmul(ps[0:n, 2 * a, h * n:(h + 1) * n], hk[a][:, h, 0:n],
                                       hg.tokens(hb, 0, a)[:, h, :], start=True, stop=True)
            ins.then_inc(hg_psum.sem, 1)
        for l in range(hg.levels):
            half = 1 << l
            for a in hg.blocks:
                pe.wait_ge(hg_q.sem, hg_q.at(hg.ev(l, a)))
                if l:
                    pe.wait_ge(hg_k.sem, hg_k.at(hg.lv(l - 1, a)))
                    pe.wait_ge(hg_s.sem, hg_s.at(hg.ev(l - 1, a)))
                right = spans(hq[a], n, half)[:, :, :, 1, :]
                for h in range(HEADS):
                    ins = nc.tensor.matmul(ps[0:n, 2 * a + (l + 1) % 2, h * (n // 2):(h + 1) * (n // 2)], hk[a][:, h, 0:n],
                                           right[:, h, :, :], start=True, stop=True)
                ins.then_inc(hg_psum.sem, 1)
        for a in hg.blocks:
            pe.wait_ge(hg_k.sem, hg_k.at(hg.lv(hg.levels - 1, a)))
            pe.wait_ge(hg_oc.sem, hg_oc.at(hg.blk0))
            pe.wait_ge(hg_state.sem, hg_state.at(8 if hg.dec else 2 * hg.blk0))
            for h in range(HEADS):
                nc.tensor.transpose(ps[0:n, 4 + a, h * P:(h + 1) * P], hk[a][:, h, 0:n], ident[:])
            for h in range(HEADS):
                ins = nc.tensor.transpose(ps[0:n, 6 + a, h * P:(h + 1) * P], hvb[a][:, h, 0:n], ident[:])
            ins.then_inc(hg_t.sem, 1)
        for a in hg.blocks:
            pe.wait_ge(hg_tn.sem, hg_tn.at(hg.blk0 + a + 1))
            pe.wait_ge(hg_s.sem, hg_s.at(hg.ev(hg.levels, a)))
            pe.wait_ge(hg_q.sem, hg_q.at(hg.ev(hg.levels, a)))
            pe.wait_ge(hg_state.sem, hg_state.at(8 if hg.dec else 2 * hg.blk0 + 2 * a))
            for h in range(HEADS):
                nc.tensor.matmul(ps[:, 4 + a, h * n:(h + 1) * n], hvn[a][0:n, h, :], hs[a][0:n, h, 0:n], start=True, stop=False)
                ins = nc.tensor.matmul(ps[:, 4 + a, h * n:(h + 1) * n], hg.state[:, h, :], hq[a][:, h, 0:n], start=False, stop=True)
            ins.then_inc(hg_o.sem, 1)
            for h in range(HEADS):
                ins = nc.tensor.matmul(ps[:, 6 + a, h * P:(h + 1) * P], hkn[a][0:n, h, :], hvn[a][0:n, h, :], start=True, stop=True)
            ins.then_inc(hg_up.sem, 1)

    def hgrn_act(act):
        act.wait_ge(mix_ready.sem, mix_ready.at(1))
        act.wait_ge(kv_stored.sem, kv_stored.at(64 * HEADS))
        act.dma_start(hmask[:], io["c_hmask"]).then_inc(hg_tables.sem, 16)
        act.dma_start(hstate[1][:], io["state_hgrn"][0, 0].rearrange("h d e -> d h e")).then_inc(hg_tables.sem, 16)
        proj_act(act, U_EVEN + 6, 4)
        act.wait_ge(hg_prep.sem, hg_prep.at(1))
        nc.scalar.activation(hlb[:, 4:8], hlb[:, 0:4], ACT.Sigmoid).then_inc(hg_gate.sem, 1)
        act.wait_ge(proj_out.sem, proj_out.at(28))
        nc.scalar.activation(hb[:, 4:8, :], hb[:, 4:8, :], ACT.Sigmoid).then_inc(hg_gate.sem, 1)
        nc.scalar.activation(hb[:, 12:16, :], hb[:, 12:16, :], ACT.Silu).then_inc(hg_gate.sem, 1)
        act.wait_ge(hg_prep.sem, hg_prep.at(2 + 2 * HEADS))
        with act.Fori(0, NB // 2) as i:
            hgrn_block_act(act, HBlock(i))
        hgrn_block_act(act, HBlock(None))
        act.wait_ge(hg_state.sem, hg_state.at(8))
        act.dma_start(io["hgrn_prompt"][0, 0].rearrange("h d e -> d h e"), hstate[0][:]).then_inc(hg_stored.sem, 16)
        act.wait_ge(hg_state.sem, hg_state.at(10))
        act.dma_start(io["hgrn_sample"][0, 0].rearrange("h d e -> d h e"), hstate[1][:]).then_inc(hg_stored.sem, 16)
        head_norm_act(act, 1, hb[:, 0:4, :], hb[:, 4:8, :], lambda e: e.wait_ge(hg_oc.sem, hg_oc.at(NB + 1)), cols[:, G3 + 1:G3 + 2], 4, 0)
        act.wait_ge(hg_stored.sem, hg_stored.at(32))

    def hgrn_dve(dve):
        nc.vector.memset(hstate[0][:], 0.0)
        lbr = cols[:, LB:LB + 8].rearrange("p (m r) -> p m r", r=2)
        nc.vector.tensor_tensor(hlb[:, 0:4], lbr[:, :, 0], lbr[:, :, 1], ALU.subtract).then_inc(hg_prep.sem, 1)
        proj_dve(dve, U_EVEN + 6, 12, 1, 4, lambda i: tile(hb, i))
        dve.wait_ge(hg_gate.sem, hg_gate.at(1))
        nc.vector.tensor_scalar(hlb[:, 8:12], hlb[:, 4:8], -1.0, 1.0, ALU.mult, ALU.add).then_inc(hg_prep.sem, 1)
        dve.wait_ge(hg_gate.sem, hg_gate.at(2))
        dve.wait_ge(hg_prep.sem, hg_prep.at(2))
        for h in range(HEADS):
            nc.vector.tensor_scalar(hb[:, 4 + h, :], hb[:, 4 + h, :], hlb[:, 8 + h:9 + h], hlb[:, 4 + h:5 + h],
                                    ALU.mult, ALU.add).then_inc(hg_prep.sem, 1)
        for h in range(HEADS):
            dve.wait_ge(hg_prep.sem, hg_prep.at(3 + h))
            nc.vector.tensor_scalar(kbuf[:, h, :], hb[:, 4 + h, :], -1.0, 1.0, ALU.mult, ALU.add).then_inc(hg_prep.sem, 1)
        dve.wait_ge(hg_tables.sem, hg_tables.at(32))
        with dve.Fori(0, NB // 2) as i:
            hgrn_block_dve(dve, HBlock(i))
        hgrn_block_dve(dve, HBlock(None))
        head_norm_dve(dve, 1, hb[:, 0:4, :], hb[:, 4:8, :], cols[:, G3 + 1:G3 + 2], 4, hb[:, 12:16, :])

    def hgrn_pool(pool):
        with pool.Fori(0, NB // 2) as i:
            hgrn_block_pool(pool, HBlock(i))
        hgrn_block_pool(pool, HBlock(None))

    def hgrn_pe(pe):
        pe.wait_ge(gn_rms.sem, gn_rms.at(1))
        proj_pe(pe, U_EVEN + 6, 12, 1, 4)
        pe.wait_ge(proj_out.sem, proj_out.at(28))
        with pe.Fori(0, NB // 2) as i:
            hgrn_block_pe(pe, HBlock(i))
        pe.wait_ge(hg_tables.sem, hg_tables.at(32))
        hgrn_block_pe(pe, HBlock(None))
        head_norm_pe(pe, 1, hb[:, 4:8, :], lambda e: (e.wait_ge(hg_oc.sem, hg_oc.at(NB + 1)), e.wait_ge(hg_state.sem, hg_state.at(10))))

    I_ODD = 28
    GB = NB + 1
    TOK0 = [b * P for b in range(NB)] + [T - P]

    def gates_pe(pe, n):
        pe.wait_ge(xl_ready.sem, xl_ready.at(8 * (n + 1)))
        pe.wait_ge(ab_lo.sem, ab_lo.at(1))
        pe.wait_ge(rstd_ready.sem, rstd_ready.at(n + 1))
        for b in range(GB):
            t0 = TOK0[b]
            for k in range(KT):
                for a, (r, w) in enumerate(((xh, wabh), (xl, wabh), (xh, wabl))):
                    ins = nc.tensor.matmul(ps[:, 0, 16 * b:16 * b + 16], r[:, k, t0:t0 + P], w[:, k, :],
                                           start=k == 0 and a == 0, stop=k == KT - 1 and a == 2)
            ins = nc.tensor.transpose(ps[:, 1, b:b + 1], rstd[0:1, t0:t0 + P], ident[0:1, 0:1])
            if b == GB - 1:
                ins.then_inc(ab_psum.sem, 1)

    def gates_act(act):
        act.dma_start(wab[:], io["odd_w_in"][0, :, 4 * D:4 * D + 16].rearrange("(k p) n -> p k n", p=P)).then_inc(ab_loaded.sem, 16)
        act.dma_start(tri0[:], io["c_tri"]).then_inc(ab_loaded.sem, 16)
        act.wait_ge(ab_loaded.sem, ab_loaded.at(32))
        nc.scalar.activation(wabh[:], wab[:], ACT.Copy).then_inc(ab_hi.sem, 1)

    def gates_act_2(act):
        act.wait_ge(gt.sem, gt.at(3))
        nc.scalar.activation(gz[:, :, :, 2], gz[:, :, :, 1], ACT.Exp)
        nc.scalar.activation(nexpa[:], adt[:, 0:8], ACT.Exp).then_inc(gta.sem, 1)
        act.wait_ge(gt.sem, gt.at(4))
        nc.scalar.activation(gz[:, :, :, 4], gz[:, :, :, 3], ACT.Ln).then_inc(gta.sem, 1)
        nc.scalar.activation(betac[:], gate_n[:, :, 8:16], ACT.Sigmoid).then_inc(gta.sem, 1)

    def gates_dve(dve):
        dve.wait_ge(ab_hi.sem, ab_hi.at(1))
        nc.vector.tensor_tensor(wabl[:], wab[:], wabh[:].bitcast(F32), ALU.subtract).then_inc(ab_lo.sem, 1)
        dve.wait_ge(ab_psum.sem, ab_psum.at(1))
        nc.vector.memset(gate_n[:], 0.0)
        nc.vector.memset(gcol[:], 0.0)
        nc.vector.tensor_copy(lcol[:, 0:GB], ps[:, 1, 0:GB]).then_inc(gt.sem, 1)
        dve.wait_ge(gt.sem, gt.at(1))
        for b in range(GB):
            src, dst = (slice(0, P), slice(0, P)) if b < NB else (slice(P - DEC, P), slice(0, DEC))
            ins = nc.vector.tensor_scalar(gate_n[dst, b, :], ps[src, 0, 16 * b:16 * b + 16], lcol[src, b:b + 1], None, ALU.mult)
        ins.then_inc(gt.sem, 1)
        dve.wait_ge(gt.sem, gt.at(2))
        nc.vector.tensor_tensor(gz[:, :, :, 0], gate_n[:, :, 0:8], adt[:, 8:16].unsqueeze(1).broadcast_to([P, GB, 8]), ALU.add).then_inc(rs_psum.sem, 1)
        dve.wait_ge(rs_psum.sem, rs_psum.at(1))
        nc.vector.scalar_tensor_tensor(out=gz[:, :, :, 1], in0=gz[:, :, :, 0], scalar=-1.0, in1=gz[:, :, :, 0], op0=ALU.mult, op1=ALU.min).then_inc(gt.sem, 1)
        dve.wait_ge(gta.sem, gta.at(1))
        nc.vector.tensor_scalar(gz[:, :, :, 3], gz[:, :, :, 2], 1.0, None, ALU.add).then_inc(gt.sem, 1)
        dve.wait_ge(gta.sem, gta.at(2))
        dve.wait_ge(gt.sem, gt.at(4))
        nc.vector.tensor_scalar(gz[:, :, :, 5], gz[:, :, :, 3], -1.0, 1.0e-8, ALU.add, ALU.max).then_inc(gt.sem, 1)
        dve.wait_ge(gt.sem, gt.at(5))
        nc.vector.reciprocal(gz[:, :, :, 3], gz[:, :, :, 5]).then_inc(gt.sem, 1)
        nc.vector.tensor_tensor(gz[:, :, :, 1], gz[:, :, :, 4], gz[:, :, :, 2], ALU.mult).then_inc(gt.sem, 1)
        dve.wait_ge(gt.sem, gt.at(7))
        nc.vector.tensor_tensor(gz[:, :, :, 4], gz[:, :, :, 1], gz[:, :, :, 3], ALU.mult).then_inc(gt.sem, 1)
        dve.wait_ge(gt.sem, gt.at(8))
        nc.vector.scalar_tensor_tensor(out=gz[:, :, :, 2], in0=gz[:, :, :, 0], scalar=0.0, in1=gz[:, :, :, 4], op0=ALU.max, op1=ALU.add).then_inc(gt.sem, 1)
        dve.wait_ge(gt.sem, gt.at(9))
        for b, n in [(b, P) for b in range(NB)] + [(NB, DEC)]:
            ins = nc.vector.scalar_tensor_tensor(out=gcol[0:n, b, :], in0=gz[0:n, b, :, 2], scalar=-1.0, in1=nexpa[0:n, :], op0=ALU.mult, op1=ALU.mult)
        ins.then_inc(gt.sem, 1)
        dve.wait_ge(gam_sum.sem, gam_sum.at(1))
        nc.vector.tensor_copy(gamc[:], ps[:, 0, 0:8 * GB].rearrange("p (b h) -> p b h", b=GB)).then_inc(gt.sem, 1)
        dve.wait_ge(gt.sem, gt.at(11))
        nc.vector.tensor_scalar(ngamc[:], gamc[:], -1.0, None, ALU.mult).then_inc(gt.sem, 1)

    def gates_pe_2(pe):
        pe.wait_ge(gt.sem, gt.at(10))
        nc.tensor.matmul(ps[:, 0, 0:8 * GB], tri0[:], gcol[:].rearrange("p b h -> p (b h)"), start=True, stop=True).then_inc(gam_sum.sem, 1)
        pe.wait_ge(gt.sem, gt.at(12))

    def conv_dve(dve, n):
        nc.vector.memset(pre[0][:, 0:3], 0.0)
        nc.vector.memset(pre[1][:, 0:3], 0.0)
        dve.wait_ge(rstd_ready.sem, rstd_ready.at(n + 1))
        u0 = U_ODD
        with dve.Fori(0, 6) as j:
            for s in range(2):
                split_lo(dve, u0 + 2 * j + s + 1, 1 - s)
                for c in range(2):
                    i = 4 * j + 2 * s + c
                    if c == 0:
                        dve.wait_ge(proj_c0.sem, proj_c0.at(I_ODD // 2 + 2 * j + s + 1))
                    else:
                        dve.wait_ge(unit_done.sem, unit_done.at(u0 + 2 * j + s + 1))
                    dve.wait_ge(tap0.sem, tap0.at(i - 1))
                    p = 2 * s + c
                    nc.vector.tensor_tensor(pre[c][:, 3:3 + TH], ps[:, 2 * p, 0:TH], rstd[:, 0:TH], ALU.mult)
                    nc.vector.tensor_tensor(pre[c][:, 3 + TH:3 + SEQ], ps[:, 2 * p + 1, 0:SEQ - TH], rstd[:, TH:SEQ], ALU.mult)
                    nc.vector.tensor_copy(pre[c][:, 3 + SEQ:6 + SEQ], cols[:, ds(7 * KT + 4 + 7 * i, 3)])
                    nc.vector.tensor_tensor(pre[c][:, 6 + SEQ:PADT], ps[:, 2 * p + 1, SEQ - TH:TH], rstd[:, SEQ:T], ALU.mult).then_inc(proj_out.sem, 1)
                    dve.wait_ge(proj_out.sem, proj_out.at(I_ODD + i + 1))
                    tail_i = dtail[:, ds(i, 1), :].rearrange("p a b -> p (a b)")
                    nc.vector.tensor_copy(tail_i[:, 0:3], pre[c][:, SEQ:3 + SEQ])
                    nc.vector.tensor_copy(tail_i[:, 3:6], pre[c][:, PADT - 3:PADT])
                    for r in range(1, CONV):
                        if r == 1:
                            dve.wait_ge(tap0.sem, tap0.at(i + 1))
                        else:
                            dve.wait_ge(tap.sem, tap.at(3 * i + r - 1))
                        nc.vector.scalar_tensor_tensor(out=cacc[c][:], in0=pre[c][:, r:r + PADT - 3], scalar=conv_col(i, r),
                                                       in1=cacc[c][:], op0=ALU.mult, op1=ALU.add).then_inc(tap.sem, 1)
        with dve.Fori(0, 2) as j:
            for s in range(2):
                split_lo(dve, u0 + 12 + 2 * j + s + 1, 1 - s)
                for c in range(2):
                    if c == 0:
                        dve.wait_ge(proj_c0.sem, proj_c0.at(I_ODD // 2 + 12 + 2 * j + s + 1))
                    else:
                        dve.wait_ge(unit_done.sem, unit_done.at(u0 + 12 + 2 * j + s + 1))
                    nc.vector.tensor_tensor(two(tile(dgate, 4 * j + 2 * s + c)), halves(2 * s + c), two(rstd[:]), ALU.mult).then_inc(proj_out.sem, 1)

    def conv_act(act):
        u0 = U_ODD
        with act.Fori(0, 6) as j:
            for s in range(2):
                split_hi(act, u0 + 2 * j + s + 1, 1 - s)
                for c in range(2):
                    i = 4 * j + 2 * s + c
                    act.wait_ge(proj_out.sem, proj_out.at(I_ODD + i + 1))
                    set_apart(act)
                    act.wait_ge(conv_done.sem, conv_done.at(i - 1))
                    set_apart(act)
                    nc.scalar.activation(cacc[c][:], pre[c][:, 0:PADT - 3], ACT.Copy, scale=conv_col(i, 0)).then_inc(tap0.sem, 1)
                    act.wait_ge(tap.sem, tap.at(3 * i + 3))
                    set_apart(act)
                    out = tile(db, i)
                    nc.scalar.activation(out[:, 0:SEQ], cacc[c][:, 0:SEQ], ACT.Silu)
                    nc.scalar.activation(out[:, SEQ:T], cacc[c][:, SEQ + 3:SEQ + 3 + DEC], ACT.Silu).then_inc(conv_done.sem, 1)
        proj_act(act, u0 + 12, 2)
        act.wait_ge(proj_out.sem, proj_out.at(I_ODD + 32))
        nc.scalar.activation(dgate[:], dgate[:], ACT.Silu).then_inc(gate_done.sem, 1)

    def l2_tiles(m):
        return db[:, 8 * (m % 2) + 4 * (m // 2):8 * (m % 2) + 4 * (m // 2) + 4, :]

    def l2_act(act):
        def square(m):
            act.wait_ge(l2_step.sem, l2_step.at(2 * (m - 1)))
            set_apart(act)
            nc.scalar.activation(l2w[m % 2][:], l2_tiles(m), ACT.Square).then_inc(l2_sq.sem, 1)
        act.wait_ge(conv_done.sem, conv_done.at(24))
        act.wait_ge(proj_out.sem, proj_out.at(I_ODD + 32))
        square(0)
        for m in range(4):
            act.wait_ge(l2_psum.sem, l2_psum.at(m + 1))
            set_apart(act)
            nc.scalar.activation(l2w[m % 2][:].rearrange("p h (a b) -> p (h a) b", a=2), ps[:, :, 0:TH], ACT.Sqrt,
                                 scale=1.0, bias=eps[:, 0:1]).then_inc(l2_rt.sem, 1)
            if m < 3:
                square(m + 1)

    def l2_pe(pe):
        for m in range(4):
            pe.wait_ge(l2_sq.sem, l2_sq.at(m + 1))
            pe.wait_ge(l2_rt.sem, l2_rt.at(m))
            for h in range(HEADS):
                for b in range(2):
                    ins = nc.tensor.matmul(ps[:, 2 * h + b, 0:TH], ones[:], l2w[m % 2][:, h, b * TH:(b + 1) * TH], start=True, stop=True)
            ins.then_inc(l2_psum.sem, 1)

    def l2_dve(dve):
        for m in range(4):
            dve.wait_ge(l2_rt.sem, l2_rt.at(m + 1))
            nc.vector.reciprocal(l2w[m % 2][:], l2w[m % 2][:]).then_inc(l2_step.sem, 1)
            dve.wait_ge(l2_step.sem, l2_step.at(2 * m + 1))
            t = l2_tiles(m).rearrange("p h t -> p (h t)")
            nc.vector.scalar_tensor_tensor(out=t, in0=t, scalar=P ** -0.5 if m % 2 == 0 else 1.0,
                                           in1=l2w[m % 2][:].rearrange("p h t -> p (h t)"), op0=ALU.mult, op1=ALU.mult).then_inc(l2_step.sem, 1)

    class DBlock:
        def __init__(self, g, b):
            self.g, self.dec = g, b is None
            self.b = NB if self.dec else b
            self.n = DEC if self.dec else BLK
            self.levels = DEC_LEVELS if self.dec else LEVELS
            self.t = GB * g + self.b
            self.lv = 33 * g + LEVELS * self.b
            self.lz = 28 * g + (LEVELS - 1) * self.b
            self.state = dstate[1] if self.dec else dstate[0]

        def tokens(self, kind):
            c0 = 8 * kind + HEADS * self.g
            if self.dec:
                return db[:, c0:c0 + HEADS, SEQ:T]
            return db[:, c0:c0 + HEADS, ds(self.b * BLK, BLK)]

        def col(self, buf, h, rows=None):
            return buf[0:self.n, ds(self.b, 1) if not self.dec else slice(NB, GB), self.g * HEADS + h:self.g * HEADS + h + 1].rearrange("p a h -> p (a h)")

        def cols4(self, buf):
            return buf[:, ds(self.b, 1) if not self.dec else slice(NB, GB), self.g * HEADS:(self.g + 1) * HEADS].rearrange("p a h -> p (a h)")

    def bank(i, n, rows=P):
        return ps[0:rows, i, 0:HEADS * n].rearrange("p (h t) -> p h t", h=HEADS)

    def delta_act(act, dl):
        n, t = dl.n, dl.t
        act.wait_ge(dl_vk.sem, dl_vk.at(t))
        set_apart(act)
        act.wait_ge(dl_kq.sem, dl_kq.at(t))
        set_apart(act)
        nc.scalar.activation(gst[:], dl.cols4(gcol).unsqueeze(2).broadcast_to([P, HEADS, BLK]), ACT.Copy)
        nc.scalar.activation(kst[:, :, 0:n], dl.tokens(1), ACT.Copy)
        nc.scalar.activation(vst[:, :, 0:n], dl.tokens(2), ACT.Copy).then_inc(dl_staged.sem, 1)
        act.wait_ge(dl_gam.sem, dl_gam.at(t + 1))
        set_apart(act)
        act.wait_ge(dl_s.sem, dl_s.at(t))
        set_apart(act)
        act.wait_ge(dl_w1.sem, dl_w1.at(t + 1))
        set_apart(act)
        nc.scalar.activation(egam[:, :, 0:n], bank(2, n), ACT.Exp).then_inc(dl_eg.sem, 1)
        for h in range(HEADS):
            nc.scalar.activation(dW[0:n, h, 0:n], dW[0:n, h, 0:n], ACT.Exp, bias=dl.col(ngamc, h))
        nc.scalar.activation(kcoef[0:n, :], kcoef[0:n, :], ACT.Exp).then_inc(dl_w2.sem, 1)
        act.wait_ge(dl_vk.sem, dl_vk.at(t + 1))
        set_apart(act)
        nc.scalar.activation(dvn[0:n], bank(3, P, n), ACT.Copy)
        act.wait_ge(dl_w3.sem, dl_w3.at(t + 1))
        set_apart(act)
        for h in range(HEADS):
            ins = nc.scalar.activation(dkn[0:n, h, :], bank(4, P, n)[:, h, :], ACT.Copy, scale=kcoef[0:n, h:h + 1])
        ins.then_inc(dl_nat.sem, 1)
        for l in range(1, dl.levels):
            act.wait_ge(dl_z.sem, dl_z.at(dl.lv + l + 1))
            set_apart(act)
            nc.scalar.activation(dZ[0:n, :, 0:n], bank(0, n, n), ACT.Copy).then_inc(dl_zc.sem, 1)
        act.wait_ge(dl_vp.sem, dl_vp.at(t + 1))
        set_apart(act)
        nc.scalar.activation(dvv[0:n], bank(4, P, n), ACT.Copy).then_inc(dl_v.sem, 1)
        act.wait_ge(dl_o.sem, dl_o.at(t + 1))
        set_apart(act)
        nc.scalar.activation(dl.tokens(0), bank(6, n), ACT.Copy).then_inc(dl_oc.sem, 1)

    def delta_pool(pool, dl):
        n, t = dl.n, dl.t
        pool.wait_ge(dl_eg.sem, dl_eg.at(t + 1))
        set_apart(pool)
        pool.wait_ge(dl_staged.sem, dl_staged.at(t + 1))
        set_apart(pool)
        pool.wait_ge(dl_o.sem, dl_o.at(t))
        set_apart(pool)
        nc.gpsimd.tensor_tensor(dkt[:, :, 0:n], kst[:, :, 0:n], egam[:, :, 0:n], ALU.mult)
        nc.gpsimd.tensor_tensor(dqt[:, :, 0:n], dl.tokens(0), egam[:, :, 0:n], ALU.mult).then_inc(dl_kq.sem, 1)
        pool.wait_ge(dl_bt.sem, dl_bt.at(t + 1))
        set_apart(pool)
        for l in range(dl.levels):
            if l == 0:
                pool.wait_ge(dl_xu.sem, dl_xu.at(dl.lv))
                set_apart(pool)
            if l >= 2:
                pool.wait_ge(dl_z.sem, dl_z.at(dl.lv + l - 1))
                set_apart(pool)
            if l == 2:
                pool.wait_ge(dl_xu.sem, dl_xu.at(dl.lv + 1))
                set_apart(pool)
            nc.gpsimd.tensor_tensor(dBl[l % 2][0:n, :, 0:n], dBT[0:n, :, 0:n],
                                    dlev[0:n, l:l + 1, 0:n].broadcast_to([n, HEADS, n]), ALU.mult).then_inc(dl_mask.sem, 1)

    def delta_dve(dve, dl):
        n, t = dl.n, dl.t
        dve.wait_ge(dl_gam.sem, dl_gam.at(t + 1))
        dve.wait_ge(dl_nat.sem, dl_nat.at(t))
        nc.vector.tensor_tensor(dW[0:n, :, 0:n], bank(2, n, n), causal[0:n, 0:n].unsqueeze(1).broadcast_to([n, HEADS, n]), ALU.add)
        nc.vector.tensor_tensor(kcoef[0:n, :], bank(2, n, n)[:, :, n - 1], dl.cols4(gamc)[0:n], ALU.subtract).then_inc(dl_w1.sem, 1)
        dve.wait_ge(dl_w2.sem, dl_w2.at(t + 1))
        for h in range(HEADS):
            nc.vector.tensor_scalar(dW[0:n, h, 0:n], dW[0:n, h, 0:n], dl.col(betac, h), None, ALU.mult)
        nc.vector.tensor_tensor(kcoef[0:n, :], kcoef[0:n, :], dl.cols4(betac)[0:n], ALU.mult).then_inc(dl_w3.sem, 1)
        dve.wait_ge(dl_kk.sem, dl_kk.at(t + 1))
        dve.wait_ge(dl_w3.sem, dl_w3.at(t + 1))
        nc.vector.tensor_tensor(dQK[0:n, :, 0:n], bank(1, n, n), dW[0:n, :, 0:n], ALU.mult)
        nc.vector.tensor_tensor(dBT[0:n, :, 0:n], bank(0, n, n), dW[0:n, :, 0:n], ALU.mult).then_inc(dl_bt.sem, 1)
        eye = ident[0:n, 0:n].unsqueeze(1).broadcast_to([n, HEADS, n])
        for l in range(dl.levels):
            if l == 0:
                dve.wait_ge(dl_mask.sem, dl_mask.at(dl.lv + 1))
                nc.vector.tensor_tensor(dU[0:n, :, 0:n], eye, dBl[0][0:n, :, 0:n], ALU.subtract)
                dve.wait_ge(dl_z.sem, dl_z.at(dl.lv + 1))
                nc.vector.tensor_tensor(dX[0:n, :, 0:n], eye, bank(0, n, n), ALU.subtract).then_inc(dl_xu.sem, 1)
                continue
            dve.wait_ge(dl_xz.sem, dl_xz.at(dl.lz + l))
            dve.wait_ge(dl_xu.sem, dl_xu.at(dl.lv + l))
            if l < dl.levels - 1:
                nc.vector.tensor_tensor(dX[0:n, :, 0:n], dX[0:n, :, 0:n], bank(1, n, n), ALU.subtract)
            nc.vector.tensor_tensor(dU[0:n, :, 0:n], dU[0:n, :, 0:n], bank(2, n, n), ALU.subtract).then_inc(dl_xu.sem, 1)
        dve.wait_ge(dl_ks.sem, dl_ks.at(t + 1))
        dve.wait_ge(dl_nat.sem, dl_nat.at(t + 1))
        nc.vector.tensor_tensor(dr[0:n], dvn[0:n], bank(3, P, n), ALU.subtract).then_inc(dl_r.sem, 1)
        dve.wait_ge(dl_up.sem, dl_up.at(t + 1))
        dve.wait_ge(dl_eg.sem, dl_eg.at(t + 1))
        for h in range(HEADS):
            ins = nc.vector.scalar_tensor_tensor(out=dl.state[:, h, :], in0=dl.state[:, h, :], scalar=egam[:, h, n - 1:n],
                                                 in1=bank(7, P)[:, h, :], op0=ALU.mult, op1=ALU.add)
        ins.then_inc(dl_s.sem, 1)

    def delta_pe(pe, dl):
        n, t = dl.n, dl.t
        pe.wait_ge(dl_staged.sem, dl_staged.at(t + 1))
        pe.wait_ge(dl_xu.sem, dl_xu.at(dl.lv))
        for h in range(HEADS):
            ins = nc.tensor.matmul(bank(2, n)[:, h, :], gst[0:n, h, :], tri[0:n, 0:n], start=True, stop=True)
        ins.then_inc(dl_gam.sem, 1)
        for h in range(HEADS):
            nc.tensor.matmul(bank(0, n, n)[:, h, :], kst[:, h, 0:n], kst[:, h, 0:n], start=True, stop=True)
            ins = nc.tensor.matmul(bank(1, n, n)[:, h, :], kst[:, h, 0:n], dl.tokens(0)[:, h, :], start=True, stop=True)
        ins.then_inc(dl_kk.sem, 1)
        pe.wait_ge(dl_r.sem, dl_r.at(t))
        pe.wait_ge(dl_v.sem, dl_v.at(t))
        for h in range(HEADS):
            nc.tensor.transpose(bank(3, P, n)[:, h, :], vst[:, h, 0:n], ident[:])
            ins = nc.tensor.transpose(bank(4, P, n)[:, h, :], kst[:, h, 0:n], ident[:])
        ins.then_inc(dl_vk.sem, 1)
        pe.wait_ge(dl_w1.sem, dl_w1.at(t + 1))
        pe.wait_ge(dl_eg.sem, dl_eg.at(t + 1))
        for l in range(dl.levels):
            pe.wait_ge(dl_mask.sem, dl_mask.at(dl.lv + l + 1))
            if l == 0:
                pe.wait_ge(dl_bt.sem, dl_bt.at(t + 1))
            else:
                pe.wait_ge(dl_xu.sem, dl_xu.at(dl.lv + l))
            for h in range(HEADS):
                ins = nc.tensor.matmul(bank(0, n, n)[:, h, :], dBl[l % 2][0:n, h, 0:n],
                                       dX[0:n, h, 0:n] if l else ident[0:n, 0:n], start=True, stop=True)
            ins.then_inc(dl_z.sem, 1)
            if l == 0:
                continue
            pe.wait_ge(dl_zc.sem, dl_zc.at(dl.lz + l))
            for h in range(HEADS):
                if l < dl.levels - 1:
                    nc.tensor.matmul(bank(1, n, n)[:, h, :], dU[0:n, h, 0:n], dZ[0:n, h, 0:n], start=True, stop=True)
                ins = nc.tensor.matmul(bank(2, n, n)[:, h, :], dZ[0:n, h, 0:n], dU[0:n, h, 0:n], start=True, stop=True)
            ins.then_inc(dl_xz.sem, 1)
        pe.wait_ge(dl_s.sem, dl_s.at(t))
        pe.wait_ge(dl_kq.sem, dl_kq.at(t + 1))
        pe.wait_ge(dl_nat.sem, dl_nat.at(t + 1))
        for h in range(HEADS):
            ins = nc.tensor.matmul(bank(3, P, n)[:, h, :], dkt[:, h, 0:n], dl.state[:, h, :], start=True, stop=True)
        ins.then_inc(dl_ks.sem, 1)
        pe.wait_ge(dl_r.sem, dl_r.at(t + 1))
        pe.wait_ge(dl_xu.sem, dl_xu.at(dl.lv + dl.levels))
        for h in range(HEADS):
            ins = nc.tensor.matmul(bank(4, P, n)[:, h, :], dU[0:n, h, 0:n], dr[0:n, h, :], start=True, stop=True)
        ins.then_inc(dl_vp.sem, 1)
        pe.wait_ge(dl_oc.sem, dl_oc.at(t))
        pe.wait_ge(dl_v.sem, dl_v.at(t + 1))
        for h in range(HEADS):
            nc.tensor.matmul(bank(6, n)[:, h, :], dl.state[:, h, :], dqt[:, h, 0:n], start=True, stop=False)
            ins = nc.tensor.matmul(bank(6, n)[:, h, :], dvv[0:n, h, :], dQK[0:n, h, 0:n], start=False, stop=True)
        ins.then_inc(dl_o.sem, 1)
        for h in range(HEADS):
            ins = nc.tensor.matmul(bank(7, P)[:, h, :], dkn[0:n, h, :], dvv[0:n, h, :], start=True, stop=True)
        ins.then_inc(dl_up.sem, 1)

    def odd_act(act, n):
        gates_act(act)
        gates_act_2(act)
        conv_act(act)
        l2_act(act)
        act.wait_ge(l2_step.sem, l2_step.at(8))
        for dst, name in ((dlev[:], "c_levels"), (causal[:], "c_causal"), (tri[:], "c_tri")):
            act.dma_start(dst, io[name]).then_inc(dl_tables.sem, 16)
        sd = io["state_delta"][0, 0].rearrange("h d e -> d h e")
        for g in range(2):
            act.wait_ge(dl_stored.sem, dl_stored.at(32 * g))
            act.dma_start(dstate[1][:], sd[:, 4 * g:4 * g + 4, :]).then_inc(dl_state_in.sem, 16)
            if g == 0:
                act.wait_ge(dl_tables.sem, dl_tables.at(48))
            with act.Fori(0, NB) as b:
                delta_act(act, DBlock(g, b))
            act.wait_ge(dl_s.sem, dl_s.at(GB * g + NB))
            act.dma_start(io["delta_prompt"][0, 0].rearrange("h d e -> d h e")[:, 4 * g:4 * g + 4, :], dstate[0][:]).then_inc(dl_stored.sem, 16)
            delta_act(act, DBlock(g, None))
            act.wait_ge(dl_s.sem, dl_s.at(GB * g + GB))
            act.dma_start(io["delta_sample"][0, 0].rearrange("h d e -> d h e")[:, 4 * g:4 * g + 4, :], dstate[1][:]).then_inc(dl_stored.sem, 16)
        for g in range(2):
            head_norm_act(act, 2 + g, db[:, 4 * g:4 * g + 4, :], db[:, 8 + 4 * g:12 + 4 * g, :], lambda e: e.wait_ge(dl_oc.sem, dl_oc.at(2 * GB)),
                          cols[:, G3 + 2:G3 + 3], 4 * g, 0)
        act.wait_ge(tail_psum.sem, tail_psum.at(1))
        nc.scalar.activation(tail_rows[:].rearrange("p (a b) -> p a b", a=6), ps[0:6, 0:6, :], ACT.Copy).then_inc(tail_copied.sem, 1)
        act.wait_ge(tail_copied.sem, tail_copied.at(1))
        act.dma_start(io["conv_prompt"][0, 0], tail_rows[0:3, :]).then_inc(tail_stored.sem, 16)
        act.dma_start(io["conv_sample"][0, 0], tail_rows[3:6, :]).then_inc(tail_stored.sem, 16)
        act.wait_ge(dl_stored.sem, dl_stored.at(64))
        act.wait_ge(tail_stored.sem, tail_stored.at(32))

    def odd_dve(dve, n):
        gates_dve(dve)
        conv_dve(dve, n)
        l2_dve(dve)
        dve.wait_ge(dl_tables.sem, dl_tables.at(48))
        for g in range(2):
            dve.wait_ge(dl_stored.sem, dl_stored.at(32 * g))
            nc.vector.memset(dstate[0][:], 0.0)
            with dve.Fori(0, NB) as b:
                delta_dve(dve, DBlock(g, b))
            dve.wait_ge(dl_state_in.sem, dl_state_in.at(16 * (g + 1)))
            delta_dve(dve, DBlock(g, None))
        dve.wait_ge(gate_done.sem, gate_done.at(1))
        for g in range(2):
            head_norm_dve(dve, 2 + g, db[:, 4 * g:4 * g + 4, :], db[:, 8 + 4 * g:12 + 4 * g, :], cols[:, G3 + 2:G3 + 3], 4 * g,
                          dgate[:, 4 * g:4 * g + 4, :])

    def odd_pool(pool):
        pool.wait_ge(l2_step.sem, l2_step.at(8))
        pool.wait_ge(dl_tables.sem, dl_tables.at(48))
        for g in range(2):
            with pool.Fori(0, NB) as b:
                delta_pool(pool, DBlock(g, b))
            delta_pool(pool, DBlock(g, None))

    def odd_pe(pe, n):
        gates_pe(pe, n)
        gates_pe_2(pe)
        proj_pe(pe, U_ODD, I_ODD, n, 8)
        pe.wait_ge(proj_out.sem, proj_out.at(I_ODD + 32))
        l2_pe(pe)
        pe.wait_ge(l2_step.sem, l2_step.at(8))
        pe.wait_ge(dl_tables.sem, dl_tables.at(48))
        for g in range(2):
            with pe.Fori(0, NB) as b:
                delta_pe(pe, DBlock(g, b))
            pe.wait_ge(dl_state_in.sem, dl_state_in.at(16 * (g + 1)))
            delta_pe(pe, DBlock(g, None))
        for g in range(2):
            head_norm_pe(pe, 2 + g, db[:, 8 + 4 * g:12 + 4 * g, :],
                         lambda e: (e.wait_ge(dl_s.sem, dl_s.at(2 * GB)), e.wait_ge(gn_rms.sem, gn_rms.at(2 + g))))
        pe.wait_ge(gn_rms.sem, gn_rms.at(4))
        for i in range(24):
            ins = nc.tensor.transpose(ps[0:6, i // 4, (i % 4) * P:(i % 4 + 1) * P], dtail[:, i, :], ident[:])
        ins.then_inc(tail_psum.sem, 1)
        pe.wait_ge(tail_copied.sem, tail_copied.at(1))

    def load_pe(pe):
        pe.wait_ge(vec_loaded.sem, vec_loaded.at(16 * VECS))
        pe.wait_ge(consts_set.sem, consts_set.at(1))
        for m in range(KT):
            nc.tensor.transpose(ps[:, 6, 7 * m:7 * m + 7], rows_gain[:, m * P:(m + 1) * P], ident[0:7, 0:7])
        for m in range(24):
            nc.tensor.transpose(ps[:, 6, 7 * (KT + m):7 * (KT + m) + 7], rows_conv[:, m * P:(m + 1) * P], ident[0:7, 0:7])
        for m in range(4):
            nc.tensor.transpose(ps[:, 6, LB + 2 * m:LB + 2 * m + 2], rows_lb[:, m * P:(m + 1) * P], ident[0:2, 0:2])
        nc.tensor.transpose(ps[:, 6, G3:G3 + 3], rows_g3[:], ident[0:3, 0:3]).then_inc(cols_psum.sem, 1)
        nc.tensor.matmul(ps[:, 7, 0:272], ones[0:1, :], row_lam[:], start=True, stop=True).then_inc(lam_psum.sem, 1)
        pe.wait_ge(in_loaded.sem, in_loaded.at(32))
        for m in range(KT):
            pe.wait_ge(x_ready.sem, x_ready.at(m - 2))
            s = m % 3
            for b in range(NB):
                nc.tensor.transpose(ps[:, 2 * s, b * P:(b + 1) * P], xnat[:, b, m * P:(m + 1) * P], ident[:])
            nc.tensor.transpose(ps[:, 2 * s + 1, 0:DEC], xnat_dec[:, m * P:(m + 1) * P],
                                ident[0:DEC, 0:DEC]).then_inc(xt_done.sem, 1)
        pe.wait_ge(lam_step.sem, lam_step.at(1))

    def load_dve(dve):
        dve.wait_ge(cols_psum.sem, cols_psum.at(1))
        nc.vector.tensor_copy(cols[:], ps[:, 6, 0:COLS]).then_inc(cols_ready.sem, 1)
        split_lo(dve, 0, 0)
        for m in range(KT):
            dve.wait_ge(xt_done.sem, xt_done.at(m + 1))
            s = m % 3
            nc.vector.tensor_copy(x[:, m, 0:SEQ], ps[:, 2 * s, :])
            nc.vector.tensor_copy(x[:, m, SEQ:T], ps[:, 2 * s + 1, 0:DEC]).then_inc(x_ready.sem, 1)
            if m:
                feed_dve(dve, 0, m - 1)
        dve.wait_ge(cols_ready.sem, cols_ready.at(1))
        feed_dve(dve, 0, KT - 1)
        dve.wait_ge(lam_psum.sem, lam_psum.at(1))
        nc.vector.tensor_copy(adt[:], ps[:, 7, 256:272])
        nc.vector.tensor_copy(lam_all[:], ps[:, 7, 0:256]).then_inc(lam_step.sem, 1)
        dve.wait_ge(lam_step.sem, lam_step.at(1))
        lam_v = lam_all[:].rearrange("p (a b c) -> p a b c", a=2, b=2)
        nc.vector.tensor_tensor(lam_prod[:], lam_v[:, :, 0, :], lam_v[:, :, 1, :], ALU.mult).then_inc(lam_step.sem, 1)
        dve.wait_ge(lam_step.sem, lam_step.at(2))
        nc.vector.reduce_sum(lamv[:, 0:2], lam_prod[:], AX_X).then_inc(lam_step.sem, 1)
        dve.wait_ge(lam_exp.sem, lam_exp.at(1))
        nc.vector.tensor_scalar(lamv[:, 4:5], lamv[:, 3:4], lamv[:, 2:3], -LAM_INIT, ALU.subtract, ALU.add).then_inc(lam_step.sem, 1)
        dve.wait_ge(lam_step.sem, lam_step.at(4))
        nc.vector.memset(lamv[0:DEC, 5:6], 1.0)
        nc.vector.tensor_copy(lamv[DEC:2 * DEC, 5:6], lamv[DEC:2 * DEC, 4:5]).then_inc(lam_step.sem, 1)
        nc.vector.tensor_scalar(lamv[:, 6:7], cols[:, G3:G3 + 1], 1.0 - LAM_INIT, None, ALU.mult).then_inc(lam_step.sem, 1)

    def output_dve(dve, n):
        stats_dve(dve, n)
        dve.wait_ge(rstd_ready.sem, rstd_ready.at(n + 1))
        for m in range(KT):
            nc.vector.scalar_tensor_tensor(out=yt[:, m, :], in0=x[:, m, :], scalar=gain(6, m), in1=rstd[:],
                                           op0=ALU.mult, op1=ALU.mult).then_inc(y_scaled.sem, 1)
        for b in range(NB + 1):
            r = P if b < NB else DEC
            dve.wait_ge(y_psum.sem, y_psum.at(b + 1))
            dve.wait_ge(y_stored[b % 2].sem, y_stored[b % 2].at(16 * (b // 2)))
            nc.vector.tensor_copy(yout[b % 2][0:r, :].rearrange("p (a n) -> p a n", a=2),
                                  ps[0:r, 2 * (b % 2):2 * (b % 2) + 2, :]).then_inc(y_copied.sem, 1)

    def output_pe(pe):
        pe.wait_ge(y_scaled.sem, y_scaled.at(KT))
        for b in range(NB + 1):
            r = P if b < NB else DEC
            pe.wait_ge(y_copied.sem, y_copied.at(b - 1))
            for m in range(KT):
                ins = nc.tensor.transpose(ps[0:r, 2 * (b % 2) + m // 4, (m % 4) * P:(m % 4 + 1) * P],
                                          yt[:, m, b * P:b * P + r], ident[:])
            ins.then_inc(y_psum.sem, 1)

    def output_act(act, n):
        stats_act(act, n)
        for b in range(NB + 1):
            act.wait_ge(y_copied.sem, y_copied.at(b + 1))
            set_apart(act)
            if b < NB:
                act.dma_start(io["y_prompt"][0, b * P:(b + 1) * P, :], yout[b % 2][:]).then_inc(y_stored[b % 2].sem, 16)
            else:
                act.dma_start(io["y_sample"][0], yout[b % 2][0:DEC, :]).then_inc(y_stored[b % 2].sem, 16)
        act.wait_ge(y_stored[0].sem, y_stored[0].at(16 * 3))
        act.wait_ge(y_stored[1].sem, y_stored[1].at(16 * 2))

    block = ctx.enter_context(nc.Block())

    @block.sync
    def _(sp):
        sp.dma_start(xnat[:], io["x_prompt"][0].rearrange("(b p) d -> p b d", p=P)).then_inc(in_loaded.sem, 16)
        sp.dma_start(xnat_dec[:], io["x_sample"][0]).then_inc(in_loaded.sem, 16)
        stream_ffn(sp, 0, io["ffn1_w_in"][0], io["ffn1_w_out"][0])
        stream_plain(sp, U_EVEN, io["even_w_in"][0], 7)
        stream_plain(sp, U_EVEN + 14, io["even_w_out"][0], 2)
        stream_ffn(sp, 1, io["ffn2_w_in"][0], io["ffn2_w_out"][0])
        stream_ffn(sp, 2, io["ffn1_w_in"][1], io["ffn1_w_out"][1])
        stream_plain(sp, U_ODD, io["odd_w_in"][0], 8)
        stream_plain(sp, U_ODD + 16, io["odd_w_out"][0], 2)
        stream_ffn(sp, 3, io["ffn2_w_in"][1], io["ffn2_w_out"][1])

    @block.scalar
    def _(act):
        for s in (hi_done, pt_copied, o_copied, tap0, conv_done, kv_stored, hg_oc, dl_nat, dl_oc, dl_v):
            s.credit_by(act)
        act.dma_start(ident[:], io["c_ident"]).then_inc(vec_loaded.sem, 16)
        for l in range(2):
            for r, name in enumerate(("ffn1_norm", "mix_norm", "ffn2_norm")):
                act.dma_start(rows_gain[3 * l + r:3 * l + r + 1, :], io[name][l:l + 1, :]).then_inc(vec_loaded.sem, 16)
        act.dma_start(rows_gain[6:7, :], io["final_norm"].rearrange("(a n) -> a n", a=1)).then_inc(vec_loaded.sem, 16)
        act.dma_start(rows_conv[0:4, :], io["conv_w"][0]).then_inc(vec_loaded.sem, 16)
        act.dma_start(rows_conv[4:7, :], io["cache_conv"][0, 0]).then_inc(vec_loaded.sem, 16)
        act.dma_start(rows_lb[:], io["hgrn_lb_logits"]).then_inc(vec_loaded.sem, 16)
        for r, name in enumerate(("diff_norm", "hgrn_norm", "delta_norm")):
            act.dma_start(rows_g3[r:r + 1, :], io[name]).then_inc(vec_loaded.sem, 16)
        act.dma_start(row_lam[:, 0:256], io["diff_lambda"].rearrange("a r d -> a (r d)")).then_inc(vec_loaded.sem, 16)
        act.dma_start(row_lam[:, 256:264], io["delta_A_log"]).then_inc(vec_loaded.sem, 16)
        act.dma_start(row_lam[:, 264:272], io["delta_dt_bias"]).then_inc(vec_loaded.sem, 16)
        split_hi(act, 0, 0)
        act.wait_ge(cols_ready.sem, cols_ready.at(1))
        for m in range(KT):
            feed_act(act, 0, m, m % 2)
        act.wait_ge(lam_step.sem, lam_step.at(3))
        nc.scalar.activation(lamv[:, 2:4], lamv[:, 0:2], ACT.Exp).then_inc(lam_exp.sem, 1)
        stats_act(act, 0)
        ffn_in_act(act, 0, 0)
        out_act(act, U_FFN[0] + 2 * FJ, OUT_PARTS, 1, False)
        stats_act(act, 1)
        att_act(act)
        hgrn_act(act)
        out_act(act, U_EVEN + 14, PLAIN_PARTS, 2, False)
        stats_act(act, 2)
        ffn_in_act(act, 1, 2)
        out_act(act, U_FFN[1] + 2 * FJ, OUT_PARTS, 3, False)
        stats_act(act, 3)
        ffn_in_act(act, 2, 3)
        out_act(act, U_FFN[2] + 2 * FJ, OUT_PARTS, 4, False)
        stats_act(act, 4)
        odd_act(act, 4)
        out_act(act, U_ODD + 16, PLAIN_PARTS, 5, False)
        stats_act(act, 5)
        ffn_in_act(act, 3, 5)
        out_act(act, U_FFN[3] + 2 * FJ, OUT_PARTS, 6, True)
        output_act(act, 6)

    @block.gpsimd
    def _(pool):
        dl_kq.credit_by(pool)
        feed_pool(pool, 0)
        ffn_in_pool(pool, 0, 0)
        feed_pool(pool, 1)
        att_pool(pool)
        hgrn_pool(pool)
        feed_pool(pool, 2)
        ffn_in_pool(pool, 1, 2)
        feed_pool(pool, 3)
        ffn_in_pool(pool, 2, 3)
        feed_pool(pool, 4)
        odd_pool(pool)
        feed_pool(pool, 5)
        ffn_in_pool(pool, 3, 5)
        feed_pool(pool, 6)

    @block.vector
    def _(dve):
        for s in (lo_done, gate_scaled, h_made, proj_out, biased, hg_s, hg_q, hg_state, dl_r, dl_s, dl_xu):
            s.credit_by(dve)
        nc.vector.memset(eps[:, 0:1], NORM_EPS)
        nc.vector.memset(eps[:, 1:2], DIFF_EPS)
        nc.vector.memset(ones[:], 1.0).then_inc(consts_set.sem, 1)
        load_dve(dve)
        stats_dve(dve, 0)
        ffn_in_dve(dve, 0, 0)
        out_dve(dve, U_FFN[0] + 2 * FJ, 0, OUT_PARTS, 1, 0.5, False)
        stats_dve(dve, 1)
        att_dve(dve)
        hgrn_dve(dve)
        out_dve(dve, U_EVEN + 14, 1, PLAIN_PARTS, 2, 1.0, False)
        stats_dve(dve, 2)
        ffn_in_dve(dve, 1, 2)
        out_dve(dve, U_FFN[1] + 2 * FJ, 2, OUT_PARTS, 3, 0.5, False)
        stats_dve(dve, 3)
        ffn_in_dve(dve, 2, 3)
        out_dve(dve, U_FFN[2] + 2 * FJ, 3, OUT_PARTS, 4, 0.5, False)
        stats_dve(dve, 4)
        odd_dve(dve, 4)
        out_dve(dve, U_ODD + 16, 4, PLAIN_PARTS, 5, 1.0, False)
        stats_dve(dve, 5)
        ffn_in_dve(dve, 3, 5)
        out_dve(dve, U_FFN[3] + 2 * FJ, 5, OUT_PARTS, 6, 0.5, True)
        output_dve(dve, 6)

    @block.tensor
    def _(pe):
        for s in (unit_done, pt_psum, o_psum, kv_t, sc_psum, hg_up, dl_o, dl_vk):
            s.credit_by(pe)
        load_pe(pe)
        stats_pe(pe, 0)
        ffn_in_pe(pe, 0, 0)
        out_pe(pe, U_FFN[0] + 2 * FJ, 0, OUT_PARTS, hh, hl, 1, hidden_ready(0))
        stats_pe(pe, 1)
        att_pe(pe)
        hgrn_pe(pe)
        out_pe(pe, U_EVEN + 14, 1, PLAIN_PARTS, mixh, mixl, 2, lambda e: e.wait_ge(mix_ready.sem, mix_ready.at(2)))
        stats_pe(pe, 2)
        ffn_in_pe(pe, 1, 2)
        out_pe(pe, U_FFN[1] + 2 * FJ, 2, OUT_PARTS, hh, hl, 3, hidden_ready(1))
        stats_pe(pe, 3)
        ffn_in_pe(pe, 2, 3)
        out_pe(pe, U_FFN[2] + 2 * FJ, 3, OUT_PARTS, hh, hl, 4, hidden_ready(2))
        stats_pe(pe, 4)
        odd_pe(pe, 4)
        out_pe(pe, U_ODD + 16, 4, PLAIN_PARTS, mixh, mixl, 5, lambda e: e.wait_ge(mix_ready.sem, mix_ready.at(4)))
        stats_pe(pe, 5)
        ffn_in_pe(pe, 3, 5)
        out_pe(pe, U_FFN[3] + 2 * FJ, 5, OUT_PARTS, hh, hl, 6, hidden_ready(3))
        stats_pe(pe, 6)
        output_pe(pe)


OUTPUTS = (
    ("y_prompt", (1, SEQ, D)), ("y_sample", (1, DEC, D)),
    ("k_prompt", (1, 1, SEQ, HEADS, 2, 64)), ("v_prompt", (1, 1, SEQ, HEADS, P)),
    ("hgrn_prompt", (1, 1, HEADS, P, P)), ("delta_prompt", (1, 1, 2 * HEADS, P, P)), ("conv_prompt", (1, 1, CONV - 1, 3 * D)),
    ("k_sample", (1, 1, DEC, HEADS, 2, 64)), ("v_sample", (1, 1, DEC, HEADS, P)),
    ("hgrn_sample", (1, 1, HEADS, P, P)), ("delta_sample", (1, 1, 2 * HEADS, P, P)), ("conv_sample", (1, 1, CONV - 1, 3 * D)),
)


def kernel(**inputs):
    import concourse.bacc as bacc
    from concourse.bass_utils import run_bass_kernel_spmd

    nc = bacc.Bacc("TRN2", target_bir_lowering=False, num_devices=1)
    arrays = {name: np.ascontiguousarray(a) for name, a in {**inputs, **constants()}.items()}
    io = {name: nc.dram_tensor(name, a.shape, mybir.dt.from_np(a.dtype), kind="ExternalInput").ap()
          for name, a in arrays.items()}
    io.update({name: nc.dram_tensor(name, shape, F32, kind="ExternalOutput").ap() for name, shape in OUTPUTS})
    program(nc, io)
    got = run_bass_kernel_spmd(nc, [arrays], core_ids=[0]).results[0]
    return tuple(got[name] for name, _ in OUTPUTS)
```
